# Optimizing a Trainium2 kernel written in Bass

```python
import math
import jax, jax.numpy as jnp
from jax import lax
import numpy as np

D_MODEL = 1024
BATCH = 1
SEQ = 256
DEPTH = 1

PLE_DIM = 256
D_POOL = 512
POOL_WINDOWS = (2, 4, 8, 16)
N_POOL_GROUPS = len(POOL_WINDOWS)
POOL_GROUP = D_POOL // N_POOL_GROUPS
D_ATTN = D_MODEL - D_POOL
N_HEADS = 8
HEAD_DIM = D_ATTN // N_HEADS
MOBA_BLOCK = 256
MOBA_TOPK = 3
Q_CHUNK = 32
NUM_BUCKETS = 32
MAX_DISTANCE = 128
D_FF = 2816
CONV_WIDTH = 3
EPS = 1e-6
D_IN = D_POOL + 3 * D_ATTN


def rms_norm(x, g):
    xf = x.astype(jnp.float32)
    y = xf * lax.rsqrt(jnp.mean(xf * xf, axis=-1, keepdims=True) + EPS)
    return (y * g.astype(jnp.float32)).astype(x.dtype)

def pool_mixer(u, w_pool, pool_scale):
    B, S, _ = u.shape
    uf = u.astype(jnp.float32)
    cpad = jnp.pad(jnp.cumsum(uf, axis=1), ((0, 0), (1, 0), (0, 0)))
    pos = jnp.arange(S)
    outs = []
    for g, w in enumerate(POOL_WINDOWS):
        c_g = cpad[:, :, g * POOL_GROUP:(g + 1) * POOL_GROUP]
        lagged = jnp.pad(c_g[:, :S + 1 - w], ((0, 0), (w - 1, 0), (0, 0)))
        count = jnp.minimum(pos + 1, w).astype(jnp.float32)[None, :, None]
        mean = (c_g[:, 1:] - lagged) / count
        outs.append(mean - uf[:, :, g * POOL_GROUP:(g + 1) * POOL_GROUP])
    pooled = jnp.stack(outs, axis=2)
    mixed = jnp.einsum('bsgc,gcd->bsgd', pooled, w_pool.astype(jnp.float32))
    return (mixed.reshape(B, S, D_POOL) * pool_scale.astype(jnp.float32)).astype(u.dtype)

def rel_bucket(dist):
    n = jnp.maximum(dist, 0)
    max_exact = NUM_BUCKETS // 2
    nf = jnp.maximum(n, 1).astype(jnp.float32)
    large = max_exact + (jnp.log(nf / max_exact) / math.log(MAX_DISTANCE / max_exact)
                         * (NUM_BUCKETS - max_exact)).astype(jnp.int32)
    large = jnp.minimum(large, NUM_BUCKETS - 1)
    return jnp.where(n < max_exact, n, large)

def moba_attention(q, k, v, rel_bias):
    B, S = q.shape[0], q.shape[1]
    nb = -(-S // MOBA_BLOCK)
    s_pad = nb * MOBA_BLOCK
    pad = ((0, 0), (0, s_pad - S), (0, 0), (0, 0))
    q, k, v = [jnp.pad(t, pad).transpose(0, 2, 1, 3) for t in (q, k, v)]
    k_blk = k.reshape(B, N_HEADS, nb, MOBA_BLOCK, HEAD_DIM)
    v_blk = v.reshape(B, N_HEADS, nb, MOBA_BLOCK, HEAD_DIM)
    k_mean = jnp.mean(k_blk.astype(jnp.float32), axis=3)
    gate = jnp.einsum('bhsd,bhnd->bhsn', q.astype(jnp.float32), k_mean)
    q_blk_idx = jnp.arange(s_pad) // MOBA_BLOCK
    past = jnp.arange(nb)[None, :] < q_blk_idx[:, None]
    gate = jnp.where(past, gate, -jnp.inf)
    n_sel = min(MOBA_TOPK, nb)
    _, sel = lax.top_k(gate, n_sel)
    sel_valid = sel < q_blk_idx[:, None]

    scale = HEAD_DIM ** -0.5
    bias_t = rel_bias.astype(jnp.float32).T
    b_idx = jnp.arange(B)[:, None, None, None]
    h_idx = jnp.arange(N_HEADS)[None, :, None, None]
    key_off = jnp.arange(MOBA_BLOCK)
    n_sel_keys = n_sel * MOBA_BLOCK

    def chunk(ci):
        start = ci * Q_CHUNK
        qc = lax.dynamic_slice_in_dim(q, start, Q_CHUNK, axis=2)
        sc = lax.dynamic_slice_in_dim(sel, start, Q_CHUNK, axis=2)
        vc = lax.dynamic_slice_in_dim(sel_valid, start, Q_CHUNK, axis=2)
        t = start + jnp.arange(Q_CHUNK)
        j = start // MOBA_BLOCK
        k_sel = k_blk[b_idx, h_idx, sc]
        v_sel = v_blk[b_idx, h_idx, sc]
        key_pos = sc[..., None] * MOBA_BLOCK + key_off
        bias_sel = bias_t[h_idx[..., None], rel_bucket(t[:, None, None] - key_pos)]
        l_sel = jnp.einsum('bhqd,bhqnkd->bhqnk', qc, k_sel).astype(jnp.float32) * scale + bias_sel
        l_sel = jnp.where(vc[..., None], l_sel, -jnp.inf)
        k_own = lax.dynamic_index_in_dim(k_blk, j, axis=2, keepdims=False)
        v_own = lax.dynamic_index_in_dim(v_blk, j, axis=2, keepdims=False)
        d_own = t[:, None] - (j * MOBA_BLOCK + key_off)[None, :]
        bias_own = bias_t[:, rel_bucket(d_own)]
        l_own = jnp.einsum('bhqd,bhkd->bhqk', qc, k_own).astype(jnp.float32) * scale + bias_own
        l_own = jnp.where(d_own >= 0, l_own, -jnp.inf)
        logits = jnp.concatenate([l_sel.reshape(B, N_HEADS, Q_CHUNK, n_sel_keys), l_own], axis=-1)
        probs = jax.nn.softmax(logits, axis=-1).astype(v.dtype)
        p_sel = probs[..., :n_sel_keys].reshape(B, N_HEADS, Q_CHUNK, n_sel, MOBA_BLOCK)
        p_own = probs[..., n_sel_keys:]
        return (jnp.einsum('bhqnk,bhqnkd->bhqd', p_sel, v_sel)
                + jnp.einsum('bhqk,bhkd->bhqd', p_own, v_own))

    outs = lax.map(chunk, jnp.arange(s_pad // Q_CHUNK))
    out = outs.transpose(1, 0, 3, 2, 4).reshape(B, s_pad, N_HEADS, HEAD_DIM)[:, :S]
    return out.reshape(B, S, D_ATTN)

def conv_ffn(h, w_up, conv_w, conv_b, w_down):
    S = h.shape[1]
    gate, val = jnp.split(h @ w_up, 2, axis=-1)
    gp = jnp.pad(gate, ((0, 0), (CONV_WIDTH - 1, 0), (0, 0)))
    conv = conv_b + gp[:, 0:S] * conv_w[0]
    for kk in range(1, CONV_WIDTH):
        conv = conv + gp[:, kk:kk + S] * conv_w[kk]
    return (jax.nn.gelu(conv, approximate=True) * val) @ w_down

def first_inputs(seed: int = 0) -> dict:
    key = jax.random.key(seed)
    ks = jax.random.split(key, 20)
    f32 = jnp.float32
    nrm = lambda k, shape, s: jax.random.normal(k, shape, f32) * s
    gain = lambda k: 1.0 + nrm(k, (DEPTH, D_MODEL), 0.05)
    return {
        "x": nrm(ks[0], (BATCH, SEQ, D_MODEL), 1.0),
        "p": nrm(ks[1], (DEPTH, BATCH, SEQ, PLE_DIM), 1.0),
        "rel_bias": nrm(ks[2], (NUM_BUCKETS, N_HEADS), 0.5),
        "g_mix_pre": gain(ks[3]),
        "g_mix_post": gain(ks[4]),
        "g_ffn_pre": gain(ks[5]),
        "g_ffn_post": gain(ks[6]),
        "w_in": nrm(ks[7], (DEPTH, D_MODEL, D_IN), D_MODEL ** -0.5),
        "w_pool": nrm(ks[8], (DEPTH, N_POOL_GROUPS, POOL_GROUP, POOL_GROUP), POOL_GROUP ** -0.5),
        "pool_scale": 1.0 + nrm(ks[9], (DEPTH, D_POOL), 0.1),
        "w_out": nrm(ks[10], (DEPTH, D_MODEL, D_MODEL), D_MODEL ** -0.5),
        "w_up": nrm(ks[11], (DEPTH, D_MODEL, 2 * D_FF), D_MODEL ** -0.5),
        "conv_w": nrm(ks[12], (DEPTH, CONV_WIDTH, D_FF), CONV_WIDTH ** -0.5),
        "conv_b": nrm(ks[13], (DEPTH, D_FF), 0.02),
        "w_down": nrm(ks[14], (DEPTH, D_FF, D_MODEL), D_FF ** -0.5),
        "w_ple": nrm(ks[15], (DEPTH, PLE_DIM, D_MODEL), PLE_DIM ** -0.5),
        "w_ple_gate": nrm(ks[16], (DEPTH, D_MODEL, D_MODEL), D_MODEL ** -0.5),
    }

def first_block(x, p, rel_bias, g_mix_pre, g_mix_post, g_ffn_pre, g_ffn_post, w_in, w_pool,
              pool_scale, w_out, w_up, conv_w, conv_b, w_down, w_ple, w_ple_gate):
    B, S, _ = x.shape
    for i in range(DEPTH):
        h = rms_norm(x, g_mix_pre[i])
        proj = h @ w_in[i]
        u, q, k, v = jnp.split(proj, [D_POOL, D_POOL + D_ATTN, D_POOL + 2 * D_ATTN], axis=-1)
        y_pool = pool_mixer(u, w_pool[i], pool_scale[i])
        y_attn = moba_attention(q.reshape(B, S, N_HEADS, HEAD_DIM),
                                k.reshape(B, S, N_HEADS, HEAD_DIM),
                                v.reshape(B, S, N_HEADS, HEAD_DIM), rel_bias)
        y = jnp.concatenate([y_pool, y_attn], axis=-1) @ w_out[i]
        x = x + rms_norm(y, g_mix_post[i])
        h = rms_norm(x, g_ffn_pre[i])
        x = x + rms_norm(conv_ffn(h, w_up[i], conv_w[i], conv_b[i], w_down[i]), g_ffn_post[i])
        x = x + (p[i] @ w_ple[i]) * jax.nn.sigmoid(x @ w_ple_gate[i])
    return x


DEPTH_2 = 2

CONV_WIDTH_2 = 512
CONV_K = 3
SWA_HEADS = 8
SWA_KV_HEADS = 2
SWA_HEAD_DIM = 64
WINDOW = 128
SWA_BLOCK = 128
GLA_HEADS = 4
GLA_DK = 64
GLA_DV = 128
GLA_GATE_RANK = 16
GLA_GATE_TAU = 16.0
GLA_CHUNK = 64
MLA_HEADS = 4
MLA_Q_RANK = 256
MLA_KV_RANK = 128
MLA_NOPE = 64
MLA_ROPE = 32
MLA_V = 128
MLA_BLOCK = 128
ROPE_THETA = 10000.0
D_FF_2 = ((-(-8 * D_MODEL // 3) + 255) // 256) * 256
ALPHA = (2.0 * DEPTH_2) ** 0.25
BETA = (8.0 * DEPTH_2) ** -0.25
LN_EPS = 1e-5
RMS_EPS = 1e-6

N_EVEN = (DEPTH_2 + 1) // 2
N_ODD = DEPTH_2 // 2

EVEN_SPLITS = [CONV_WIDTH_2, CONV_WIDTH_2, CONV_WIDTH_2,
               SWA_HEADS * SWA_HEAD_DIM, SWA_KV_HEADS * SWA_HEAD_DIM, SWA_KV_HEADS * SWA_HEAD_DIM]
EVEN_IN = sum(EVEN_SPLITS)
EVEN_MIX = CONV_WIDTH_2 + SWA_HEADS * SWA_HEAD_DIM
ODD_SPLITS = [GLA_HEADS * GLA_DK, GLA_HEADS * GLA_DK, GLA_HEADS * GLA_DV, GLA_GATE_RANK,
              GLA_HEADS * GLA_DV, MLA_Q_RANK, MLA_KV_RANK, MLA_ROPE]
ODD_IN = sum(ODD_SPLITS)
ODD_MIX = GLA_HEADS * GLA_DV + MLA_HEADS * MLA_V


def split_cols(u, sizes):
    return jnp.split(u, np.cumsum(sizes)[:-1].tolist(), axis=-1)

def layer_norm(x, g, b):
    xf = x.astype(jnp.float32)
    mu = xf.mean(-1, keepdims=True)
    var = jnp.mean(jnp.square(xf - mu), -1, keepdims=True)
    return ((xf - mu) * lax.rsqrt(var + LN_EPS) * g.astype(jnp.float32) + b.astype(jnp.float32)).astype(x.dtype)

def rms_norm_2(x, g):
    xf = x.astype(jnp.float32)
    ms = jnp.mean(jnp.square(xf), -1, keepdims=True)
    return (xf * lax.rsqrt(ms + RMS_EPS) * g.astype(jnp.float32)).astype(x.dtype)

def apply_rope(t, cos, sin):
    t1, t2 = jnp.split(t, 2, axis=-1)
    return jnp.concatenate([t1 * cos - t2 * sin, t2 * cos + t1 * sin], axis=-1)

def short_conv_mixer(b_gate, c_gate, h, conv_w):
    S = h.shape[1]
    z = c_gate * h
    zp = jnp.pad(z, ((0, 0), (CONV_K - 1, 0), (0, 0)))
    y = zp[:, 0:S] * conv_w[0]
    for j in range(1, CONV_K):
        y = y + zp[:, j:j + S] * conv_w[j]
    return b_gate * y

def swa_sink_attention(q, k, v, sinks):
    B_, S, _ = q.shape
    nb = S // SWA_BLOCK
    G = SWA_HEADS // SWA_KV_HEADS
    q = q.reshape(B_, nb, SWA_BLOCK, SWA_KV_HEADS, G, SWA_HEAD_DIM)
    k = k.reshape(B_, nb, SWA_BLOCK, SWA_KV_HEADS, SWA_HEAD_DIM)
    v = v.reshape(B_, nb, SWA_BLOCK, SWA_KV_HEADS, SWA_HEAD_DIM)
    pad = ((0, 0), (1, 0), (0, 0), (0, 0), (0, 0))
    kk = jnp.concatenate([jnp.pad(k, pad)[:, :-1], k], axis=2)
    vv = jnp.concatenate([jnp.pad(v, pad)[:, :-1], v], axis=2)
    s = jnp.einsum('bnqhgd,bnkhd->bnhgqk', q, kk).astype(jnp.float32) * (SWA_HEAD_DIM ** -0.5)
    qi = jnp.arange(SWA_BLOCK)[:, None]
    kj = jnp.arange(2 * SWA_BLOCK)[None, :] - SWA_BLOCK
    diff = qi - kj
    band = (diff >= 0) & (diff < WINDOW)
    valid = (jnp.arange(nb)[:, None, None] > 0) | (kj[None] >= 0)
    mask = band[None] & valid
    s = jnp.where(mask[None, :, None, None], s, -jnp.inf)
    sink = sinks.astype(jnp.float32).reshape(SWA_KV_HEADS, G)[None, None, :, :, None, None]
    m = jnp.maximum(s.max(-1, keepdims=True), sink)
    p = jnp.exp(s - m)
    p = p / (p.sum(-1, keepdims=True) + jnp.exp(sink - m))
    o = jnp.einsum('bnhgqk,bnkhd->bnqhgd', p.astype(v.dtype), vv)
    return o.reshape(B_, S, SWA_HEADS * SWA_HEAD_DIM)

def gla_mixer(q, k, v, g_low, r, w_gate, b_gate, g_norm):
    B_, S, _ = q.shape
    H, C = GLA_HEADS, GLA_CHUNK
    nc = S // C
    log_a = jax.nn.log_sigmoid((g_low @ w_gate + b_gate).astype(jnp.float32)) / GLA_GATE_TAU

    def to_chunks(t, d):
        return t.astype(jnp.float32).reshape(B_, nc, C, H, d).transpose(1, 0, 3, 2, 4)

    qc = to_chunks(q, GLA_DK) * (GLA_DK ** -0.5)
    kc = to_chunks(k, GLA_DK)
    vc = to_chunks(v, GLA_DV)
    gc = to_chunks(log_a, GLA_DK)
    causal = jnp.tril(jnp.ones((C, C), bool))[:, :, None]

    def step(state, inp):
        qb, kb, vb, gb = inp
        b = jnp.cumsum(gb, axis=2)
        o_inter = jnp.einsum('bhtd,bhdv->bhtv', qb * jnp.exp(b), state)
        diff = b[:, :, :, None, :] - b[:, :, None, :, :]
        decay = jnp.exp(jnp.where(causal, diff, -jnp.inf))
        attn = jnp.einsum('bhtd,bhsd,bhtsd->bhts', qb, kb, decay)
        o = o_inter + jnp.einsum('bhts,bhsv->bhtv', attn, vb)
        b_last = b[:, :, -1:, :]
        k_dec = kb * jnp.exp(b_last - b)
        state = jnp.exp(b_last[:, :, 0, :])[..., None] * state + jnp.einsum('bhsd,bhsv->bhdv', k_dec, vb)
        return state, o

    s0 = jnp.zeros((B_, H, GLA_DK, GLA_DV), jnp.float32)
    _, o = lax.scan(step, s0, (qc, kc, vc, gc))
    o = o.transpose(1, 0, 3, 2, 4).reshape(B_, S, H, GLA_DV)
    o = rms_norm_2(o, g_norm).reshape(B_, S, H * GLA_DV)
    return (o * jax.nn.silu(r.astype(jnp.float32))).astype(q.dtype)

def mla_mixer(c_q, c_kv, k_r, g_qn, w_uq, g_kvn, w_ukv, cos, sin):
    B_, S, _ = c_q.shape
    H = MLA_HEADS
    q = (rms_norm_2(c_q, g_qn) @ w_uq).reshape(B_, S, H, MLA_NOPE + MLA_ROPE)
    q_nope = q[..., :MLA_NOPE]
    q_rope = apply_rope(q[..., MLA_NOPE:], cos[:, None, :], sin[:, None, :])
    kv = (rms_norm_2(c_kv, g_kvn) @ w_ukv).reshape(B_, S, H, MLA_NOPE + MLA_V)
    k_nope, v = kv[..., :MLA_NOPE], kv[..., MLA_NOPE:]
    k_rope = apply_rope(k_r, cos, sin)
    scale = (MLA_NOPE + MLA_ROPE) ** -0.5
    nb = S // MLA_BLOCK
    qn_b = q_nope.reshape(B_, nb, MLA_BLOCK, H, MLA_NOPE).transpose(1, 0, 2, 3, 4)
    qr_b = q_rope.reshape(B_, nb, MLA_BLOCK, H, MLA_ROPE).transpose(1, 0, 2, 3, 4)
    kpos = jnp.arange(S)

    def attend(args):
        qn, qr, i = args
        s = (jnp.einsum('bqhd,bkhd->bhqk', qn, k_nope) +
             jnp.einsum('bqhr,bkr->bhqk', qr, k_rope)).astype(jnp.float32) * scale
        qpos = i * MLA_BLOCK + jnp.arange(MLA_BLOCK)
        s = jnp.where(kpos[None, :] <= qpos[:, None], s, -jnp.inf)
        p = jax.nn.softmax(s, axis=-1)
        return jnp.einsum('bhqk,bkhv->bqhv', p.astype(v.dtype), v)

    o = lax.map(attend, (qn_b, qr_b, jnp.arange(nb)))
    return o.transpose(1, 0, 2, 3, 4).reshape(B_, S, H * MLA_V)

def swiglu(x, w_gate, w_up, w_down):
    return (jax.nn.silu(x @ w_gate) * (x @ w_up)) @ w_down

def second_inputs(seed: int = 0) -> dict:
    key = jax.random.key(seed)
    ks = iter(jax.random.split(key, 32))
    nrm = lambda shape, s: jax.random.normal(next(ks), shape, jnp.float32) * s
    D = D_MODEL
    return {
        "x": nrm((BATCH, SEQ, D), 1.0),
        "ev_w_in": nrm((N_EVEN, D, EVEN_IN), D ** -0.5),
        "ev_conv_w": nrm((N_EVEN, CONV_K, CONV_WIDTH_2), CONV_K ** -0.5),
        "ev_sinks": nrm((N_EVEN, SWA_HEADS), 0.5),
        "ev_w_out": nrm((N_EVEN, EVEN_MIX, D), BETA * EVEN_MIX ** -0.5),
        "od_w_in": nrm((N_ODD, D, ODD_IN), D ** -0.5),
        "od_gla_w_gate": nrm((N_ODD, GLA_GATE_RANK, GLA_HEADS * GLA_DK), GLA_GATE_RANK ** -0.5),
        "od_gla_b_gate": nrm((N_ODD, GLA_HEADS * GLA_DK), 0.1),
        "od_gla_norm_g": 1.0 + nrm((N_ODD, GLA_DV), 0.02),
        "od_mla_q_norm_g": 1.0 + nrm((N_ODD, MLA_Q_RANK), 0.02),
        "od_mla_w_uq": nrm((N_ODD, MLA_Q_RANK, MLA_HEADS * (MLA_NOPE + MLA_ROPE)), MLA_Q_RANK ** -0.5),
        "od_mla_kv_norm_g": 1.0 + nrm((N_ODD, MLA_KV_RANK), 0.02),
        "od_mla_w_ukv": nrm((N_ODD, MLA_KV_RANK, MLA_HEADS * (MLA_NOPE + MLA_V)), MLA_KV_RANK ** -0.5),
        "od_w_out": nrm((N_ODD, ODD_MIX, D), BETA * ODD_MIX ** -0.5),
        "ffn_w_gate": nrm((DEPTH_2, D, D_FF_2), D ** -0.5),
        "ffn_w_up": nrm((DEPTH_2, D, D_FF_2), D ** -0.5),
        "ffn_w_down": nrm((DEPTH_2, D_FF_2, D), BETA * D_FF_2 ** -0.5),
        "ln_mix_g": 1.0 + nrm((DEPTH_2, D), 0.02),
        "ln_mix_b": nrm((DEPTH_2, D), 0.02),
        "ln_ffn_g": 1.0 + nrm((DEPTH_2, D), 0.02),
        "ln_ffn_b": nrm((DEPTH_2, D), 0.02),
    }

def second_block(x, ev_w_in, ev_conv_w, ev_sinks, ev_w_out, od_w_in, od_gla_w_gate, od_gla_b_gate,
              od_gla_norm_g, od_mla_q_norm_g, od_mla_w_uq, od_mla_kv_norm_g, od_mla_w_ukv, od_w_out,
              ffn_w_gate, ffn_w_up, ffn_w_down, ln_mix_g, ln_mix_b, ln_ffn_g, ln_ffn_b):
    S = x.shape[1]
    pos = jnp.arange(S, dtype=jnp.float32)
    inv_freq = ROPE_THETA ** (-jnp.arange(0, MLA_ROPE, 2, dtype=jnp.float32) / MLA_ROPE)
    ang = pos[:, None] * inv_freq[None, :]
    cos, sin = jnp.cos(ang).astype(x.dtype), jnp.sin(ang).astype(x.dtype)

    for layer in range(DEPTH_2):
        i = layer // 2
        if layer % 2 == 0:
            u = x @ ev_w_in[i]
            b_g, c_g, h, q, k, v = split_cols(u, EVEN_SPLITS)
            ya = short_conv_mixer(b_g, c_g, h, ev_conv_w[i])
            yb = swa_sink_attention(q, k, v, ev_sinks[i])
            y = jnp.concatenate([ya, yb], axis=-1) @ ev_w_out[i]
        else:
            u = x @ od_w_in[i]
            gq, gk, gv, g_low, gr, c_q, c_kv, k_r = split_cols(u, ODD_SPLITS)
            yc = gla_mixer(gq, gk, gv, g_low, gr, od_gla_w_gate[i], od_gla_b_gate[i], od_gla_norm_g[i])
            yd = mla_mixer(c_q, c_kv, k_r, od_mla_q_norm_g[i], od_mla_w_uq[i],
                           od_mla_kv_norm_g[i], od_mla_w_ukv[i], cos, sin)
            y = jnp.concatenate([yc, yd], axis=-1) @ od_w_out[i]
        x = layer_norm(ALPHA * x + y, ln_mix_g[layer], ln_mix_b[layer])
        x = layer_norm(ALPHA * x + swiglu(x, ffn_w_gate[layer], ffn_w_up[layer], ffn_w_down[layer]),
                       ln_ffn_g[layer], ln_ffn_b[layer])
    return x


def setup_inputs(seed=0):
    out = dict(first_inputs(seed))
    for name, value in second_inputs(seed + 1).items():
        if name != "x":
            out[name + "_2"] = value
    return out


def reference(
    x, p, rel_bias, g_mix_pre, g_mix_post, g_ffn_pre, g_ffn_post, w_in, w_pool, pool_scale,
    w_out, w_up, conv_w, conv_b, w_down, w_ple, w_ple_gate, ev_w_in_2, ev_conv_w_2, ev_sinks_2,
    ev_w_out_2, od_w_in_2, od_gla_w_gate_2, od_gla_b_gate_2, od_gla_norm_g_2, od_mla_q_norm_g_2,
    od_mla_w_uq_2, od_mla_kv_norm_g_2, od_mla_w_ukv_2, od_w_out_2, ffn_w_gate_2, ffn_w_up_2,
    ffn_w_down_2, ln_mix_g_2, ln_mix_b_2, ln_ffn_g_2, ln_ffn_b_2,
):
    x = first_block(
        x, p, rel_bias, g_mix_pre, g_mix_post, g_ffn_pre, g_ffn_post, w_in, w_pool, pool_scale,
        w_out, w_up, conv_w, conv_b, w_down, w_ple, w_ple_gate,
    )
    return second_block(
        x, ev_w_in_2, ev_conv_w_2, ev_sinks_2, ev_w_out_2, od_w_in_2, od_gla_w_gate_2,
        od_gla_b_gate_2, od_gla_norm_g_2, od_mla_q_norm_g_2, od_mla_w_uq_2, od_mla_kv_norm_g_2,
        od_mla_w_ukv_2, od_w_out_2, ffn_w_gate_2, ffn_w_up_2, ffn_w_down_2, ln_mix_g_2,
        ln_mix_b_2, ln_ffn_g_2, ln_ffn_b_2,
    )


_drawn_inputs = setup_inputs


def setup_inputs(seed=0):
    import zlib

    import numpy as np

    out = dict(_drawn_inputs(seed))
    spreads = {}
    factors = {'conv_b': 3.52,
     'ev_sinks_2': 8.0,
     'od_gla_w_gate_2': 3.902,
     'od_gla_b_gate_2': 8.0,
     'od_gla_norm_g_2': 8.0,
     'od_mla_q_norm_g_2': 8.0,
     'od_mla_kv_norm_g_2': 8.0}
    for name, (base, spread) in spreads.items():
        noise = np.random.default_rng([zlib.crc32(name.encode()), seed]).standard_normal(out[name].shape)
        drawn = base * np.exp(spread * noise) if base else spread * noise
        out[name] = __import__('jax').numpy.asarray(drawn.astype(out[name].dtype))
    for name, factor in factors.items():
        out[name] = (out[name] * factor).astype(out[name].dtype)
    return out
```

```python
from contextlib import ExitStack
import math

import numpy as np

import concourse.bass as bass
from concourse import mybir

F32 = mybir.dt.float32
F32R = mybir.dt.float32r
U8 = mybir.dt.uint8
ALU = mybir.AluOpType
ACT = mybir.ActivationFunctionType
AX_X = mybir.AxisListType.X

P = 128
SEQ = 256
D = 1024
NCH = D // P
PLE = 256
HEADS, DH = 8, 64
D_FF = 2816
NFF = D_FF // P
ALPHA = 4.0 ** 0.25
RMS_EPS, LN_EPS = 1e-6, 1e-5
BUCKETS, MAX_DISTANCE = 32, 128
GLA_H, GLA_CHUNK, GLA_TAU = 4, 64, 16.0
MLA_H, MLA_QK = 4, 96
NEG = -1e30
UNIT = 1024
SLOTS = 6

U_IN = 0
U_OUT = U_IN + 16
U_FFN1 = U_OUT + 8
U_PLE = U_FFN1 + 3 * NFF
U_EV_IN = U_PLE + 10
U_EV_OUT = U_EV_IN + 18
U_FFN2 = U_EV_OUT + 8
U_OD_IN = U_FFN2 + 3 * NFF
U_MLA = U_OD_IN + 16
U_OD_OUT = U_MLA + 2
U_FFN3 = U_OD_OUT + 8
UNITS = U_FFN3 + 3 * NFF

VEC, _at = {}, 0
for _name, _n in (("g_mix_pre", 8), ("g_mix_post", 8), ("g_ffn_pre", 8), ("g_ffn_post", 8),
                  ("pool_scale", 4), ("conv_w", 3 * NFF), ("conv_b", NFF), ("ev_conv_w", 12),
                  ("ln_mix_g", 16), ("ln_mix_b", 16), ("ln_ffn_g", 16), ("ln_ffn_b", 16),
                  ("b_gate", 2), ("gla_g", 1), ("q_g", 2), ("kv_g", 1), ("sinks", 8)):
    VEC[_name] = _at
    _at += _n
N_VEC = _at
LEVELS = (0, 1, 2, 4, 8, 16, 32, 64)


class Cursor:

    def __init__(self):
        self.n, self.turn, self.per = 0, None, 0

    def at(self, more=0):
        n = self.n + more
        return n if self.turn is None else self.turn * self.per + n

    def enter(self, turn, per):
        self.turn, self.per, self.start = turn, per, self.n

    def leave(self, turns):
        assert self.n - self.start == self.per, (self.n, self.start, self.per)
        self.n, self.turn = self.start + self.per * turns, None


class Chain:

    def __init__(self, eng, sem):
        self.eng, self.sem, self.count = eng, sem, Cursor()

    def done(self, ins):
        self.count.n += 1
        return ins.then_inc(self.sem, 1)

    def settle(self):
        self.eng.wait_ge(self.sem, self.count.at())


def build(nc, d, out):
    with ExitStack() as ctx:
        def sb(name, shape, dt=F32):
            return ctx.enter_context(nc.sbuf_tensor(name, shape, dt))

        def sem(name):
            return ctx.enter_context(nc.semaphore(name))

        raw = sb("raw", [P, SLOTS, UNIT])
        w_hi = sb("w_hi", [P, SLOTS, UNIT], F32R)
        w_lo = sb("w_lo", [P, SLOTS, UNIT], F32R)
        x = sb("x", [P, NCH, SEQ])
        op_hi = sb("op_hi", [P, NCH, SEQ], F32R)
        op_lo = sb("op_lo", [P, NCH, SEQ], F32R)
        mix_hi = sb("mix_hi", [P, NCH, SEQ], F32R)
        mix_lo = sb("mix_lo", [P, NCH, SEQ], F32R)
        y = sb("y", [P, NCH, SEQ])
        sq = sb("sq", [P, NCH, SEQ])
        proj = sb("proj", [P, 16, SEQ])
        vtok = sb("vtok", [P, 2, 512])
        root = sb("root", [P, 512])
        rinv = sb("rinv", [P, 512])
        bias = sb("bias", [P, HEADS, 384])
        logit = sb("logit", [P, 2, 384])
        probT = sb("probT", [P, 2, 384])
        stat = sb("stat", [P, 2, 8])
        work = sb("work", [P, 17, SEQ])
        vec = sb("vec", [P, N_VEC])
        ident = sb("ident", [P, P])
        flip = sb("flip", [P, P])
        mean_w = sb("mean_w", [P, 3, P])
        eps = sb("eps", [P, 2])
        wpool = sb("wpool", [P, 4, P])
        w_gate = sb("w_gate", [16, 256])
        rel = sb("rel", [BUCKETS + 1, HEADS])
        invc = sb("invc", [P, 4, 16])
        masks = sb("masks", [P, 2, 384])
        rope = sb("rope", [P, SEQ])
        gmask = sb("gmask", [P, len(LEVELS), P], U8)
        scan0 = sb("scan0", [P, SEQ])
        pt = sb("pt", [P, 2, SEQ])
        ps = ctx.enter_context(nc.psum_tensor("ps", [P, 8, 512], F32))
        scratch = nc.dram_tensor("bias_rows", (HEADS, 384), F32, kind="Internal")

        gmask_f = proj[:, 12:16, :].rearrange("p a b -> p (a b)").rearrange("p (l k) -> p l k", l=len(LEVELS))
        skew = y
        strip = work[0:BUCKETS + 1, 15:17, 0:192]
        table = work[0:HEADS, 13:15, 0:192]
        pads = work[:, 0:13, :].rearrange("p a b -> p (a b)")[:, 0:12 * (16 + SEQ)] \
            .rearrange("p (k c t) -> p k c t", k=3, c=4)
        u_pad, pad_b, pad_c = pads[:, 0], pads[:, 1], pads[:, 2]
        h_hi, h_lo = mix_hi[:, 0:2, :], mix_lo[:, 0:2, :]
        p_hi, p_lo = mix_hi[:, 2:4, :], mix_lo[:, 2:4, :]
        h_fp, gate, conv = proj[:, 0:2, :], proj[:, 2:4, :], proj[:, 4:6, :]
        flat = work[:, :, :].rearrange("p a b -> p (a b)")
        att = flat[:, 0:1024].rearrange("p (a b) -> p a b", a=2)
        gb, gd, ge = flat[:, 1024:1536], flat[:, 1536:2048], flat[:, 2048:2560]
        gqk = flat[:, 2560:3584].rearrange("p (a b) -> p a b", a=2)
        cross = flat[:, 3584:4096].rearrange("p (a b) -> p a b", a=2)
        wide = bias[:, :, :].rearrange("p a b -> p (a b)")
        mq = wide[:, 0:1024].rearrange("p (h t) -> p h t", h=4)
        mk = wide[:, 1024:2048].rearrange("p (h t) -> p h t", h=4)
        mv = wide[:, 2048:3072].rearrange("p (t n) -> p t n", t=2)
        swa_k = y[:, 0, :]

        names = """x_loaded consts_loaded pool_const table_ready table_copied table_stored skew_loaded
            flip_done bias_copied split_hi_done split_done units_done sq_ready stat_done root_ready
            x_ready norm_fp norm_hi operand_ready acc_free z_ready centred evac
            pooled pool_mixed mix_ready scores_done logits_done shift_ready probs_done probs_scaled
            probT_done probT_copied heads_done gate_scaled conv_done gate_act h_ready
            p_hi_done p_split sig_done gate_z gate_zb softplus_done decay_ready decay_exp decayed
            level_done level_kept cross_kept gla_out gla_sq gla_stat gla_root
            mla_sq mla_stat mla_root mla_normed mla_hi mla_split rope_done mla_evac
            act_step dve_step out_stored""".split()
        S = {n: sem(n) for n in names}
        raw_loaded = [sem(f"raw_loaded_{s}") for s in range(SLOTS)]
        EV_IN, EV_EVEN, EV_ODD = 0, 14, 14 + 19
        POOL_CONSTS, X_END = 9, 28

        def bank(b, a=0, n=512):
            return ps[:, b, a:a + n]

        def chunk(b, c):
            return ps[:, b, c * SEQ:c * SEQ + SEQ]

        def acc(c):
            return chunk(c // 2, c % 2)

        def pair(t, i):
            return t[:, 2 * i:2 * i + 2, :]

        def bank2(b):
            return ps[:, b, :].rearrange("p (c t) -> p c t", c=2)

        def vcol(name, c, n=1):
            at = VEC[name] + c
            return vec[:, at:at + n]

        def fp(ap):
            return ap.bitcast(F32)

        def over(ap, n):
            return ap.unsqueeze(1).to_broadcast([ap.shape[0], n, ap.shape[1]])

        block = ctx.enter_context(nc.Block())

        @block.sync
        def _(sp):
            for s in range(SLOTS):
                sp.dma_start(raw[:, s, :], d["stream"][s]).then_inc(raw_loaded[s], 16)
            rounds = UNITS // SLOTS
            with sp.Fori(1, rounds) as r:
                at = [sp.snap(r * SLOTS + s) for s in range(SLOTS)]
                for s in range(SLOTS):
                    sp.wait_ge(S["split_done"], r * SLOTS + (s - SLOTS + 1))
                    sp.dma_start(raw[:, s, :], d["stream"][bass.ds(at[s], 1)].rearrange("a p n -> p (a n)")
                                 ).then_inc(raw_loaded[s], 16)
            for v in range(rounds * SLOTS, UNITS):
                sp.wait_ge(S["split_done"], v - SLOTS + 1)
                sp.dma_start(raw[:, v % SLOTS, :], d["stream"][v]).then_inc(raw_loaded[v % SLOTS], 16)
            sp.wait_ge(S["x_ready"], X_END)
            sp.dma_start(out, x[:]).then_inc(S["out_stored"], 16)
            sp.wait_ge(S["out_stored"], 16)

        consts = [("rel", rel[:]), ("strip", strip), ("vec", vec[:]), ("flip", flip[:]), ("wpool", wpool[:]),
                  ("ident", ident[:]), ("invc", invc[:]), ("masks", masks[:]), ("p", pt[:]), ("rope", rope[:]),
                  ("gmask", gmask_f), ("scan0", scan0[:]), ("w_gate", w_gate[:])]

        @block.gpsimd
        def _(pool):
            pool.memset(mean_w[:, 0, :], 1.0 / D).then_inc(S["pool_const"], 1)
            pool.memset(mean_w[:, 1, :], 1.0 / 256).then_inc(S["pool_const"], 1)
            pool.memset(mean_w[:, 2, :], 1.0 / 128).then_inc(S["pool_const"], 1)
            pool.memset(eps[:, 0:1], RMS_EPS).then_inc(S["pool_const"], 1)
            pool.memset(eps[:, 1:2], LN_EPS).then_inc(S["pool_const"], 1)
            pool.memset(pad_b[:, :, 0:16], 0.0).then_inc(S["pool_const"], 1)
            pool.memset(pad_c[:, :, 0:16], 0.0).then_inc(S["pool_const"], 1)
            pool.memset(u_pad[:, :, 0:16], 0.0).then_inc(S["pool_const"], 1)
            pool.wait_ge(S["consts_loaded"], 16 * len(consts))
            pool.tensor_copy(gmask[:], gmask_f).then_inc(S["pool_const"], 1)
            pool.wait_ge(S["table_copied"], 1)
            pool.dma_start(scratch.ap().rearrange("h (a b) -> h a b", a=2), table).then_inc(S["table_stored"], 16)
            pool.wait_ge(S["table_stored"], 16)
            pool.dma_start(skew[:], bass.AP(scratch, 0, [[1, P], [384, HEADS], [1, SEQ]])
                           ).then_inc(S["skew_loaded"], 16)

        @block.tensor
        def _(pe):
            unit, sq_count, hidden, head_count = Cursor(), Cursor(), Cursor(), Cursor()

            def take():
                pe.wait_ge(S["split_done"], unit.at(1))
                return unit.n % SLOTS

            def given(last):
                last.then_inc(S["units_done"], 1)
                unit.n += 1

            def three(o, wh, wl, xh, xl, start, stop, **kw):
                pe.matmul(o, wh, xh, start=start, stop=False, **kw)
                pe.matmul(o, wh, xl, start=False, stop=False, **kw)
                return pe.matmul(o, wl, xh, start=False, stop=stop, **kw)

            def out_chunk(o, operand=None):
                s = take()
                for k in range(NCH):
                    if operand is not None and k % 2 == 0:
                        pe.wait_ge(S["operand_ready"], 4 * operand + k // 2 + 1)
                    w = slice(k * P, k * P + P)
                    m = three(o, w_hi[:, s, w], w_lo[:, s, w], op_hi[:, k, :], op_lo[:, k, :], k == 0, k == NCH - 1)
                given(m)

            def in_chunk(xh, xl, first, last):
                s = take()
                for c in range(NCH):
                    w = slice(c * P, c * P + P)
                    m = three(acc(c), w_hi[:, s, w], w_lo[:, s, w], xh, xl, first and c % 2 == 0, last,
                              skip_group_check=True)
                given(m)

            def token_unit(n, xh, xl, k0, kn, last, s=None, col=0, banks=(4, 5)):
                s = take()
                for k in range(kn):
                    w = slice(k * n, k * n + n)
                    for t in range(2):
                        tok = slice(t * P, t * P + P)
                        o = bank(banks[t], 0, n)
                        a, b = xh[:, k0 + k, tok], xl[:, k0 + k, tok]
                        pe.matmul(o, a, w_hi[:, s, w], start=k0 + k == 0, stop=False)
                        pe.matmul(o, a, w_lo[:, s, w], start=False, stop=False)
                        m = pe.matmul(o, b, w_hi[:, s, w], start=False, stop=last and k == kn - 1)
                given(m)

            def mean_over_features(b, src, ready):
                for piece in range(4):
                    pe.wait_ge(S[ready], ready_base[ready] + piece + 1)
                    for c in (2 * piece, 2 * piece + 1):
                        m = pe.matmul(chunk(b, 0), mean_w[:, 0, :], src[:, c, :], start=c == 0, stop=c == NCH - 1)
                m.then_inc(S["stat_done"], 1)
                ready_base[ready] += 4
            ready_base = {"sq_ready": 0, "z_ready": 0}

            def feed_forward(operand):
                def up(c, wait=None):
                    out_chunk(chunk(4 + 2 * c, 0), wait)
                    out_chunk(chunk(5 + 2 * c, 0))

                def down(c, j, first=False, last=False):
                    pe.wait_ge(S["h_ready"], j)
                    in_chunk(h_hi[:, c, :], h_lo[:, c, :], first, last)

                j = hidden.n
                up(0, operand)
                up(1, operand)
                down(0, j + 1, first=True)
                up(0)
                down(1, j + 2)
                up(1)
                turns = NFF // 2 - 2
                with pe.Fori(0, turns) as i:
                    unit.enter(i, 6)
                    down(0, i * 2 + (j + 3))
                    up(0)
                    down(1, i * 2 + (j + 4))
                    up(1)
                    unit.leave(turns)
                down(0, j + NFF - 1)
                down(1, j + NFF, last=True)
                hidden.n += NFF

            def attention(n, q, k, v, o, fillers, mixed):
                h0 = head_count.n
                order = [c for f in fillers for c in f]

                def scores(h):
                    g, b = h0 + h, 4 + (h0 + h) % 2
                    if g >= 2:
                        pe.wait_ge(S["logits_done"], g - 1)
                    pe.matmul(bank(b, 0, P), q(h)[:, 0:P], k(h)[:, 0:P], start=True, stop=True)
                    pe.matmul(bank(b, P, SEQ), q(h)[:, P:SEQ], k(h), start=True, stop=True
                              ).then_inc(S["scores_done"], 1)

                def turn(h):
                    g = h0 + h
                    pe.wait_ge(S["probs_scaled"], g + 1)
                    if g:
                        pe.wait_ge(S["probT_copied"], g)
                    for j in range(3):
                        m = pe.transpose(bank(6, j * P, P), logit[:, g % 2, j * P:j * P + P], ident[:])
                    m.then_inc(S["probT_done"], 1)

                def values(h):
                    g = h0 + h
                    lo, free = o(h)
                    pe.wait_ge(S["probT_copied"], g + 1)
                    if free is not None:
                        pe.wait_ge(S["mix_ready"], free)
                    pe.matmul(ps[lo:lo + v(h, 0).shape[1], 7, 0:SEQ], v(h, 0), probT[:, g % 2, 0:SEQ],
                              start=True, stop=False, skip_group_check=True)
                    pe.matmul(ps[lo:lo + v(h, 0).shape[1], 7, P:SEQ], v(h, 1), probT[:, g % 2, SEQ:384],
                              start=False, stop=True, skip_group_check=True).then_inc(S["heads_done"], 1)

                for t in range(n + 2):
                    if t < n:
                        scores(t)
                    if 1 <= t <= n:
                        turn(t - 1)
                    for c in fillers[t]:
                        pe.wait_ge(S["mix_ready"], mixed + c + 1)
                        in_chunk(mix_hi[:, c, :], mix_lo[:, c, :], c == order[0], c == order[-1])
                    if 1 <= t <= n:
                        values(t - 1)
                head_count.n += n

            pe.wait_ge(S["consts_loaded"], 16 * len(consts))
            pe.wait_ge(S["pool_const"], POOL_CONSTS)
            pe.matmul(ps[0:HEADS, 7, 0:384], rel[:], strip, start=True, stop=True).then_inc(S["table_ready"], 1)
            mean_over_features(6, sq, "sq_ready")
            pe.wait_ge(S["skew_loaded"], 16)
            for h in range(HEADS):
                if h >= 4:
                    pe.wait_ge(S["bias_copied"], h - 3)
                pe.matmul(bank(h % 4, 0, P), flip[:], skew[:, h, P:SEQ], start=True, stop=True)
                pe.matmul(bank(h % 4, P, SEQ), flip[:], skew[:, h, :], start=True, stop=True
                          ).then_inc(S["flip_done"], 1)

            for c in range(12):
                if c < 4:
                    pe.wait_ge(S["bias_copied"], 5 + c)
                else:
                    pe.wait_ge(S["evac"], EV_IN + c - 3)
                out_chunk(chunk(c % 4, 0), 0 if c == 0 else None)
            for i in range(4):
                token_unit(512, op_hi, op_lo, 2 * i, 2, i == 3)
            pe.wait_ge(S["pooled"], 1)
            pe.wait_ge(S["root_ready"], 1)
            for g in range(4):
                m = pe.matmul(chunk(6 + g // 2, g % 2), wpool[:, g, :], proj[:, g, :], start=True, stop=True)
            m.then_inc(S["pool_mixed"], 1)
            pe.wait_ge(S["evac"], EV_IN + 14)
            attention(
                HEADS,
                q=lambda h: proj[h % 2 * 64:h % 2 * 64 + 64, 4 + h // 2, :],
                k=lambda h: proj[h % 2 * 64:h % 2 * 64 + 64, 8 + h // 2, :],
                v=lambda h, t: vtok[:, t, h * 64:h * 64 + 64],
                o=lambda h: (h % 2 * 64, 4 + h // 2 if h % 2 == 0 else None),
                fillers=[[], [0], [1], [2], [3], [4], [5], [], [6], [7]], mixed=0)
            mean_over_features(4, sq, "sq_ready")
            mean_over_features(5, sq, "sq_ready")
            pe.wait_ge(S["root_ready"], 3)
            pe.wait_ge(S["acc_free"], 1)
            feed_forward(1)
            mean_over_features(4, sq, "sq_ready")
            pe.wait_ge(S["acc_free"], 2)
            pe.wait_ge(S["p_split"], 1)
            for c in range(2):
                in_chunk(p_hi[:, c, :], p_lo[:, c, :], c == 0, c == 1)
            pe.wait_ge(S["root_ready"], 4)
            for c in range(NCH):
                if c >= 4:
                    pe.wait_ge(S["sig_done"], c - 3)
                out_chunk(chunk(4 + c % 4, 0), 2)
            for c in range(17):
                if c >= 4:
                    pe.wait_ge(S["evac"], EV_EVEN + c - 3)
                out_chunk(chunk(c % 4, 0), 3)
            token_unit(128, op_hi, op_lo, 0, 8, True)
            pe.wait_ge(S["evac"], EV_EVEN + 19)
            attention(
                HEADS,
                q=lambda h: proj[h % 2 * 64:h % 2 * 64 + 64, 12 + h // 2, :],
                k=lambda h: swa_k[h % 2 * 64:h % 2 * 64 + 64, :],
                v=lambda h, t: vtok[:, t, h % 2 * 64:h % 2 * 64 + 64],
                o=lambda h: (h % 2 * 64, 12 + h // 2 if h % 2 == 0 else None),
                fillers=[[], [0], [1], [2], [3], [4], [5], [], [6], [7]], mixed=8)
            mean_over_features(4, y, "z_ready")
            mean_over_features(5, sq, "sq_ready")
            feed_forward(4)
            mean_over_features(4, y, "z_ready")
            mean_over_features(5, sq, "sq_ready")
            def level(i, m):
                if m:
                    pe.wait_ge(S["decayed"], i)
                if i:
                    pe.wait_ge(S["level_kept"], i)
                else:
                    pe.wait_ge(S["evac"], EV_ODD + 8)
                    pe.wait_ge(S["gate_zb"], 1)
                    pe.wait_ge(S["mla_root"], 1)
                for a in range(2):
                    for h in range(2):
                        r = slice(h * 64, h * 64 + 64)
                        for t in range(2):
                            if m:
                                at = a * SEQ + t * P
                                kk = qq = gqk[r, i % 2, at:at + P]
                            else:
                                kk, qq = proj[r, 6 + a, t * P:t * P + P], proj[r, 4 + a, t * P:t * P + P]
                            mm = pe.matmul(bank(6 + h, (2 * a + t) * P, P), kk, qq, start=True, stop=True)
                mm.then_inc(S["level_done"], 1)

            for c in range(12):
                if c >= 4:
                    pe.wait_ge(S["evac"], EV_ODD + c - 3)
                if c == 8:
                    pe.wait_ge(S["evac"], EV_ODD + 3)
                    for a in range(2):
                        m = pe.matmul(chunk(7, a), w_gate[:, a * P:a * P + P], proj[0:16, 2, :], start=True, stop=True)
                    m.then_inc(S["gate_z"], 1)
                    pe.wait_ge(S["mla_sq"], 1)
                    pe.matmul(chunk(6, 0), mean_w[:, 1, :], sq[:, 4, :], start=True, stop=False)
                    pe.matmul(chunk(6, 0), mean_w[:, 1, :], sq[:, 5, :], start=False, stop=True)
                    pe.matmul(chunk(6, 1), mean_w[:, 2, :], sq[:, 6, :], start=True, stop=True
                              ).then_inc(S["mla_stat"], 1)
                if c == 10:
                    level(0, LEVELS[0])
                out_chunk(chunk(c % 4, 0), 5)
            level(1, LEVELS[1])
            for i in range(4):
                token_unit(512, op_hi, op_lo, 2 * i, 2, i == 3)
                level(2 + i, LEVELS[2 + i])
            s = take()
            pe.wait_ge(S["mla_split"], 1)
            pe.wait_ge(S["evac"], EV_ODD + 14)
            for h in range(MLA_H):
                for k in range(2):
                    w = slice(k * 512 + h * P, k * 512 + h * P + P)
                    m = three(chunk(h // 2, h % 2), w_hi[:, s, w], w_lo[:, s, w], mix_hi[:, 4 + k, :],
                              mix_lo[:, 4 + k, :], k == 0, k == 1)
            given(m)
            s = take()
            for h in range(MLA_H):
                w = slice(h * P, h * P + P)
                three(chunk(2 + h // 2, h % 2), w_hi[:, s, w], w_lo[:, s, w], mix_hi[:, 6, :], mix_lo[:, 6, :], True, True)
            for t in range(2):
                a, b = mix_hi[:, 6, t * P:t * P + P], mix_lo[:, 6, t * P:t * P + P]
                pe.matmul(bank(4 + t), a, w_hi[:, s, 512:1024], start=True, stop=False)
                pe.matmul(bank(4 + t), a, w_lo[:, s, 512:1024], start=False, stop=False)
                m = pe.matmul(bank(4 + t), b, w_hi[:, s, 512:1024], start=False, stop=True)
            given(m)
            level(6, LEVELS[6])
            level(7, LEVELS[7])
            pe.wait_ge(S["decayed"], 8)
            pe.wait_ge(S["level_kept"], 8)
            for a in range(2):
                for h in range(2):
                    r = slice(h * 64, h * 64 + 64)
                    m = pe.matmul(bank(6 + h, a * P, P), gqk[r, 0, a * SEQ:a * SEQ + P],
                                  gqk[r, 0, a * SEQ + P:a * SEQ + SEQ], start=True, stop=True)
            m.then_inc(S["level_done"], 1)
            pe.wait_ge(S["cross_kept"], 1)
            for h in range(GLA_H):
                a, r = h // 2, h % 2
                v0, v1 = vtok[:, 0, h * P:h * P + P], vtok[:, 1, h * P:h * P + P]
                pe.matmul(bank(6 + a, r * SEQ, P), v0, att[:, r, 2 * a * P:2 * a * P + P], start=True, stop=True)
                pe.matmul(bank(6 + a, r * SEQ + P, P), v1, att[:, r, (2 * a + 1) * P:(2 * a + 2) * P],
                          start=True, stop=False)
                m = pe.matmul(bank(6 + a, r * SEQ + P, P), v0, cross[:, r, a * P:a * P + P], start=False, stop=True)
            m.then_inc(S["gla_out"], 1)
            pe.wait_ge(S["mla_evac"], 3)
            for a in range(2):
                pe.wait_ge(S["gla_sq"], a + 1)
                pe.matmul(bank(4 + a), mean_w[:, 2, :], sq[:, 2 * a:2 * a + 2, :], start=True, stop=True
                          ).then_inc(S["gla_stat"], 1)
            pe.wait_ge(S["gla_root"], 2)
            pe.wait_ge(S["rope_done"], 1)
            attention(
                MLA_H,
                q=lambda h: mq[0:MLA_QK, h, :], k=lambda h: mk[0:MLA_QK, h, :],
                v=lambda h, t: mv[:, t, h * P:h * P + P],
                o=lambda h: (0, 20 + h),
                fillers=[[], [0], [1], [2], [3], [4, 5, 6, 7]], mixed=16)
            mean_over_features(4, y, "z_ready")
            mean_over_features(5, sq, "sq_ready")
            feed_forward(6)
            mean_over_features(4, y, "z_ready")
            mean_over_features(5, sq, "sq_ready")
            assert unit.n == UNITS

        @block.scalar
        def _(act):
            own = Chain(act, S["act_step"])
            unit, split, stats, roots, sq_n, xs, ops, hidden, head_count, evac = (Cursor() for _ in range(10))

            def split_hi():
                s, turn = split.n % SLOTS, split.n // SLOTS
                act.wait_ge(raw_loaded[s], 16 * turn + 16 if split.turn is None else split.turn * 16 + (16 * turn + 16))
                if split.turn is not None or split.n >= SLOTS:
                    act.wait_ge(S["units_done"], split.at(1 - SLOTS))
                act.activation(w_hi[:, s, :], raw[:, s, :], ACT.Copy).then_inc(S["split_hi_done"], 1)
                split.n += 1

            def step(ahead=True):
                if ahead:
                    split_hi()
                unit.n += 1

            def unit_done():
                act.wait_ge(S["units_done"], unit.at())

            def squares(i, src):
                act.activation(pair(sq, i), src, ACT.Square).then_inc(S["sq_ready"], 1)

            def take_root(b, e, n=SEQ):
                stats.n += 1
                act.wait_ge(S["stat_done"], stats.n)
                act.activation(root[:, 0:n], bank(b, 0, n), ACT.Sqrt, bias=eps[:, e:e + 1]).then_inc(S["root_ready"], 1)

            def operand_hi(src, ready):
                for i in range(4):
                    act.wait_ge(S[ready], xs.n + i + 1 if ready == "x_ready" else ops_fp[0] + i + 1)
                    act.activation(pair(op_hi, i), pair(src, i), ACT.Copy).then_inc(S["norm_hi"], 1)
                if ready == "norm_fp":
                    ops_fp[0] += 4
            ops_fp = [0]

            def copy_out(dst, src, func=ACT.Copy, scale=1.0):
                act.activation(dst, src, func, scale=scale).then_inc(S["evac"], 1)

            def probs(g, sink=None):
                r = g % 2
                act.wait_ge(S["shift_ready"], g + 1)
                act.activation(logit[:, r, 0:P], logit[:, r, 0:P], ACT.Exp, bias=stat[:, r, 0:1],
                               accum_out=stat[:, r, 2:3])
                if sink is not None:
                    act.activation(stat[:, r, 6:8], stat[:, r, 0:2], ACT.Exp, bias=vcol("sinks", sink))
                act.activation(logit[:, r, P:384], logit[:, r, P:384], ACT.Exp, bias=stat[:, r, 1:2],
                               accum_out=stat[:, r, 3:4]).then_inc(S["probs_done"], 1)

            def attention(n, fillers, sink=None):
                h0 = head_count.n
                for t in range(n + 2):
                    if t < n:
                        probs(h0 + t, sink and sink(t))
                    for _ in range(fillers[t]):
                        step()
                    if 1 <= t <= n:
                        g = h0 + t - 1
                        act.wait_ge(S["probT_done"], g + 1)
                        if g >= 2:
                            act.wait_ge(S["heads_done"], g - 1)
                        act.activation(probT[:, g % 2, :], bank(6, 0, 384), ACT.Copy).then_inc(S["probT_copied"], 1)
                head_count.n += n

            def feed_forward(convolve, late=0):
                j0 = hidden.n

                def hidden_chunk(c, j, up=True):
                    step(ahead=not skip[0])
                    skip[0] -= skip[0] > 0
                    if not convolve:
                        unit_done()
                        act.activation(gate[:, c, :], chunk(4 + 2 * c, 0), ACT.Silu).then_inc(S["gate_act"], 1)
                    else:
                        unit_done()
                        act.activation(conv[:, c, :], chunk(4 + 2 * c, 0), ACT.Identity,
                                       scale=wcol(2 * NFF, j), bias=wcol(3 * NFF, j)).then_inc(S["gate_scaled"], 1)
                    step(ahead=not skip[0])
                    skip[0] -= skip[0] > 0
                    if convolve:
                        act.wait_ge(S["conv_done"], j + 1)
                        act.activation(gate[:, c, :], conv[:, c, :], ACT.Gelu_apprx_tanh).then_inc(S["gate_act"], 1)

                def wcol(at, j):
                    return vec[:, bass.ds(j + (VEC["conv_w"] + at), 1)] if not isinstance(j, int) else \
                        vec[:, j + VEC["conv_w"] + at:j + VEC["conv_w"] + at + 1]

                skip = [late]
                hidden_chunk(0, 0)
                hidden_chunk(1, 1)
                step()
                hidden_chunk(0, 2)
                step()
                hidden_chunk(1, 3)
                turns = NFF // 2 - 2
                with act.Fori(0, turns) as i:
                    unit.enter(i, 6)
                    split.enter(i, 6)
                    step()
                    hidden_chunk(0, i * 2 + 4)
                    step()
                    hidden_chunk(1, i * 2 + 5)
                    unit.leave(turns)
                    split.leave(turns)
                step(ahead=not late)
                step(ahead=not late)
                hidden.n = j0 + NFF

            def layer_norm_squares():
                stats.n += 1
                for i in range(4):
                    act.wait_ge(S["centred"], ln[0] * 4 + i + 1)
                    squares(i, pair(y, i))
                ln[0] += 1
                take_root(5, 1)
            ln = [0]

            act.dma_start(x[:], d["x"]).then_inc(S["x_loaded"], 16)
            for name, ap in consts:
                act.dma_start(ap, d[name]).then_inc(S["consts_loaded"], 16)
            act.wait_ge(S["x_loaded"], 16)
            for i in range(4):
                squares(i, pair(x, i))
            for _ in range(4):
                split_hi()
            act.wait_ge(S["pool_const"], POOL_CONSTS)
            take_root(6, 0)
            operand_hi(sq, "norm_fp")
            for h in range(HEADS):
                act.wait_ge(S["flip_done"], h + 1)
                act.activation(bias[:, h, :], bank(h % 4, 0, 384), ACT.Copy).then_inc(S["bias_copied"], 1)
            for c in range(12):
                step()
                unit_done()
                copy_out(u_pad[:, c, 16:] if c < 4 else proj[:, c, :], chunk(c % 4, 0))
            for i in range(4):
                step()
            unit_done()
            for t in range(2):
                copy_out(vtok[:, t, :], bank(4 + t))
            attention(HEADS, [0, 1, 1, 1, 1, 1, 1, 0, 1, 1])

            unit_done()
            for b in range(4):
                squares(b, bank2(b))
            take_root(4, 0)
            for i in range(4):
                act.wait_ge(S["x_ready"], i + 1)
                squares(i, pair(x, i))
            xs.n += 4
            take_root(5, 0)
            operand_hi(sq, "norm_fp")
            act.activation(p_hi, pt[:], ACT.Copy).then_inc(S["p_hi_done"], 1)
            feed_forward(True)
            unit_done()
            for b in range(4):
                squares(b, bank2(b))
            take_root(4, 0)
            operand_hi(x, "x_ready")
            xs.n += 4
            step()
            step()
            for c in range(NCH):
                step()
                unit_done()
                act.activation(sq[:, c, :], chunk(4 + c % 4, 0), ACT.Sigmoid).then_inc(S["sig_done"], 1)
            operand_hi(x, "x_ready")
            xs.n += 4
            for c in range(17):
                step()
                unit_done()
                copy_out(proj[:, c, :] if c < 16 else swa_k, chunk(c % 4, 0))
            step()
            unit_done()
            for t in range(2):
                copy_out(vtok[:, t, 0:P], bank(4 + t, 0, P))
            attention(HEADS, [0, 1, 1, 1, 1, 1, 1, 0, 1, 1], sink=lambda h: h // 2 + 4 * (h % 2))
            layer_norm_squares()
            operand_hi(x, "x_ready")
            xs.n += 4
            feed_forward(False)
            layer_norm_squares()
            operand_hi(x, "x_ready")
            xs.n += 4
            def decay(i):
                act.wait_ge(S["decay_ready"], i)
                if i > 1:
                    act.wait_ge(S["decayed"], i - 1)
                act.activation(ge, gd, ACT.Exp, scale=1.0 / GLA_TAU).then_inc(S["decay_exp"], 1)

            for c in range(12):
                step()
                unit_done()
                copy_out(proj[:, c, :], chunk(c % 4, 0), ACT.Silu if c >= 8 else ACT.Copy,
                         0.125 if c in (4, 5) else 1.0)
                if c == 4:
                    act.wait_ge(S["evac"], EV_ODD + 4)
                    own.done(act.activation(sq[:, 4:6, :], proj[:, 0:2, :], ACT.Square))
                    act.activation(sq[:, 6, :], proj[:, 3, :], ACT.Square).then_inc(S["mla_sq"], 1)
                if c == 8:
                    act.wait_ge(S["mla_stat"], 1)
                    act.activation(root[:], bank(6), ACT.Sqrt, bias=eps[:, 0:1]).then_inc(S["mla_root"], 1)
                    act.wait_ge(S["gate_zb"], 1)
                    own.done(act.activation(ge, gd, ACT.Abs))
                    own.settle()
                    own.done(act.activation(ge, ge, ACT.Exp, scale=-1.0))
                    own.settle()
                    act.activation(ge, ge, ACT.Ln, bias=1.0).then_inc(S["softplus_done"], 1)
                if c == 10:
                    act.wait_ge(S["mla_normed"], 1)
                    act.activation(mix_hi[:, 4:7, :], y[:, 0:3, :], ACT.Copy).then_inc(S["mla_hi"], 1)
                if c == 11:
                    decay(1)
            for i in range(4):
                step()
                decay(2 + i)
            unit_done()
            for t in range(2):
                copy_out(vtok[:, t, :], bank(4 + t))
            step()
            unit_done()
            for b in range(2):
                m = act.activation(mq[0:64, 2 * b:2 * b + 2, :], ps[0:64, b, :].rearrange("p (c t) -> p c t", c=2), ACT.Copy)
            m.then_inc(S["mla_evac"], 1)
            step()
            decay(6)
            unit_done()
            for b in range(2):
                m = act.activation(mk[0:64, 2 * b:2 * b + 2, :], ps[0:64, 2 + b, :].rearrange("p (c t) -> p c t", c=2), ACT.Copy)
            m.then_inc(S["mla_evac"], 1)
            for b in range(2):
                m = act.activation(mv[:, b, :], bank(4 + b), ACT.Copy)
            m.then_inc(S["mla_evac"], 1)
            decay(7)
            decay(8)
            act.wait_ge(S["gla_out"], 1)
            for a in range(2):
                act.activation(pair(sq, a), bank2(6 + a), ACT.Square).then_inc(S["gla_sq"], 1)
            for a in range(2):
                act.wait_ge(S["gla_stat"], a + 1)
                if a:
                    act.wait_ge(S["mix_ready"], 18)
                act.activation(root[:], bank(4 + a), ACT.Sqrt, bias=eps[:, 0:1]).then_inc(S["gla_root"], 1)
            attention(MLA_H, [0, 1, 1, 1, 1, 4])
            layer_norm_squares()
            operand_hi(x, "x_ready")
            xs.n += 4
            feed_forward(False, late=2)
            layer_norm_squares()
            assert unit.n == UNITS and split.n == UNITS, (unit.n, split.n)

        @block.vector
        def _(dve):
            own = Chain(dve, S["dve_step"])
            unit, split, roots, ops, hidden, head_count, ln = (Cursor() for _ in range(7))
            hi_n, means, sqs = [0], [0], [4]

            def split_lo():
                s = split.n % SLOTS
                dve.wait_ge(S["split_hi_done"], split.at(1))
                dve.tensor_tensor(w_lo[:, s, :], raw[:, s, :], fp(w_hi[:, s, :]), ALU.subtract
                                  ).then_inc(S["split_done"], 1)
                split.n += 1

            def step(ahead=True):
                if ahead:
                    split_lo()
                unit.n += 1

            def unit_done():
                dve.wait_ge(S["units_done"], unit.at())

            def chained(ins):
                own.done(ins)
                own.settle()

            def invert_root(n=SEQ):
                roots.n += 1
                dve.wait_ge(S["root_ready"], roots.n)
                chained(dve.reciprocal(rinv[:, 0:n], root[:, 0:n]))

            def operand_lo(src):
                for i in range(4):
                    dve.wait_ge(S["norm_hi"], hi_n[0] + i + 1)
                    dve.tensor_tensor(pair(op_lo, i), pair(src, i), fp(pair(op_hi, i)), ALU.subtract
                                      ).then_inc(S["operand_ready"], 1)
                hi_n[0] += 4

            def pre_norm(gain):
                invert_root()
                for i in range(4):
                    for c in (2 * i, 2 * i + 1):
                        m = dve.scalar_tensor_tensor(sq[:, c, :], x[:, c, :], vcol(gain, c), rinv[:, 0:SEQ],
                                                     ALU.mult, ALU.mult)
                    m.then_inc(S["norm_fp"], 1)
                operand_lo(sq)

            def post_norm(gain):
                for b in range(4):
                    dve.wait_ge(S["sq_ready"], sqs[0] + b + 1)
                    for c in (2 * b, 2 * b + 1):
                        m = dve.tensor_scalar(y[:, c, :], acc(c), vcol(gain, c), None, ALU.mult)
                    if b < 3:
                        own.done(m)
                m.then_inc(S["acc_free"], 1)
                acc_n[0] += 1
                dve.wait_ge(S["acc_free"], acc_n[0])
                sqs[0] += 8
                invert_root()
                for i in range(4):
                    own.done(dve.tensor_tensor(pair(y, i), pair(y, i), over(rinv[:, 0:SEQ], 2), ALU.mult))
                own.settle()
                for i in range(4):
                    dve.tensor_tensor(pair(x, i), pair(x, i), pair(y, i), ALU.add).then_inc(S["x_ready"], 1)
            acc_n = [0]

            def layer_norm(gain, shift, layer):
                l0 = ln.n
                for b in range(4):
                    dve.scalar_tensor_tensor(pair(y, b), pair(x, b), ALPHA, bank2(b), ALU.mult, ALU.add
                                             ).then_inc(S["z_ready"], 1)
                ln.n += 4
                means[0] += 1
                dve.wait_ge(S["z_ready"], ln.n)
                dve.wait_ge(S["stat_done"], stat_at[means[0] - 1])
                for i in range(4):
                    dve.tensor_tensor(pair(y, i), pair(y, i), over(chunk(4, 0), 2), ALU.subtract
                                      ).then_inc(S["centred"], 1)
                invert_root()
                dve.wait_ge(S["centred"], ln.n)
                for i in range(4):
                    own.done(dve.tensor_tensor(pair(y, i), pair(y, i), over(rinv[:, 0:SEQ], 2), ALU.mult))
                own.settle()
                for i in range(4):
                    for c in (2 * i, 2 * i + 1):
                        m = dve.tensor_scalar(x[:, c, :], y[:, c, :], vcol(gain, layer * 8 + c),
                                              vcol(shift, layer * 8 + c), ALU.mult, ALU.add)
                    m.then_inc(S["x_ready"], 1)
            stat_at = [5, 7, 9, 11]

            def put_mix(c, n, src, hi_scale=None):
                hi, lo = mix_hi[:, c:c + n, :], mix_lo[:, c:c + n, :]
                chained(dve.tensor_copy(hi, src))
                dve.tensor_tensor(lo, src, fp(hi), ALU.subtract).then_inc(S["mix_ready"], n)

            def logits(g, tile, scale, sink):
                r = g % 2
                dve.wait_ge(S["scores_done"], g + 1)
                if g >= 2:
                    dve.wait_ge(S["probT_done"], g - 1)
                dve.scalar_tensor_tensor(logit[:, r, :], bank(4 + r, 0, 384), scale, tile, ALU.mult, ALU.add
                                         ).then_inc(S["logits_done"], 1)
                dve.wait_ge(S["logits_done"], g + 1)
                own.done(dve.reduce_max(stat[:, r, 0:1], logit[:, r, 0:P], AX_X))
                chained(dve.reduce_max(stat[:, r, 1:2], logit[:, r, P:384], AX_X))
                if sink is None:
                    m = dve.tensor_scalar(stat[:, r, 0:2], stat[:, r, 0:2], -1.0, None, ALU.mult)
                else:
                    m = dve.tensor_scalar(stat[:, r, 0:2], stat[:, r, 0:2], vcol("sinks", sink), -1.0, ALU.max, ALU.mult)
                m.then_inc(S["shift_ready"], 1)

            def normalise(g, sink):
                r = g % 2
                dve.wait_ge(S["probs_done"], g + 1)
                if sink is not None:
                    chained(dve.tensor_tensor(stat[:, r, 2:4], stat[:, r, 2:4], stat[:, r, 6:8], ALU.add))
                chained(dve.reciprocal(stat[:, r, 4:6], stat[:, r, 2:4]))
                own.done(dve.tensor_scalar(logit[:, r, 0:P], logit[:, r, 0:P], stat[:, r, 4:5], None, ALU.mult))
                dve.tensor_scalar(logit[:, r, P:384], logit[:, r, P:384], stat[:, r, 5:6], None, ALU.mult
                                  ).then_inc(S["probs_scaled"], 1)

            def attention(n, tile, scale, fillers, per_chunk, sink=None):
                h0 = head_count.n
                for t in range(n + 2):
                    if t < n:
                        logits(h0 + t, tile(t), scale, sink and sink(t))
                    if 1 <= t <= n:
                        normalise(h0 + t - 1, sink and sink(t - 1))
                    for _ in range(fillers[t]):
                        step()
                    if t >= 2 and (t - 1) % per_chunk == 0:
                        dve.wait_ge(S["heads_done"], h0 + t - 1)
                        put_mix(4 + (t - 1) // per_chunk - 1, 1, ps[:, 7:8, 0:SEQ])
                head_count.n += n

            def feed_forward(convolve, late=0):
                j0 = hidden.n
                skip = [late]

                def wcol(at, j):
                    return vec[:, bass.ds(j + (VEC["conv_w"] + at), 1)] if not isinstance(j, int) else \
                        vec[:, j + VEC["conv_w"] + at:j + VEC["conv_w"] + at + 1]

                def hidden_chunk(c, j):
                    for _ in range(2):
                        step(ahead=not skip[0])
                        skip[0] -= skip[0] > 0
                    if convolve:
                        dve.wait_ge(S["gate_scaled"], j + 1)
                        g = ps[:, 4 + 2 * c, 0:SEQ]
                        chained(dve.scalar_tensor_tensor(conv[:, c, 1:], g[:, 0:SEQ - 1], wcol(NFF, j), conv[:, c, 1:],
                                                         ALU.mult, ALU.add))
                        dve.scalar_tensor_tensor(conv[:, c, 2:], g[:, 0:SEQ - 2], wcol(0, j), conv[:, c, 2:],
                                                 ALU.mult, ALU.add).then_inc(S["conv_done"], 1)
                    unit_done()
                    dve.wait_ge(S["gate_act"], j + (j0 + 1))
                    chained(dve.tensor_tensor(h_fp[:, c, :], gate[:, c, :], chunk(5 + 2 * c, 0), ALU.mult))
                    chained(dve.tensor_copy(h_hi[:, c, :], h_fp[:, c, :]))
                    dve.tensor_tensor(h_lo[:, c, :], h_fp[:, c, :], fp(h_hi[:, c, :]), ALU.subtract
                                      ).then_inc(S["h_ready"], 1)

                hidden_chunk(0, 0)
                hidden_chunk(1, 1)
                step()
                hidden_chunk(0, 2)
                step()
                hidden_chunk(1, 3)
                turns, per = NFF // 2 - 2, 4 + 2 * convolve
                with dve.Fori(0, turns) as i:
                    unit.enter(i, 6)
                    split.enter(i, 6)
                    own.count.enter(i, per)
                    step()
                    hidden_chunk(0, i * 2 + 4)
                    step()
                    hidden_chunk(1, i * 2 + 5)
                    unit.leave(turns)
                    split.leave(turns)
                    own.count.leave(turns)
                step(ahead=not late)
                step(ahead=not late)
                hidden.n = j0 + NFF

            dve.wait_ge(S["table_ready"], 1)
            dve.tensor_copy(table, ps[0:HEADS, 7, 0:384].rearrange("h (a b) -> h a b", a=2)).then_inc(S["table_copied"], 1)
            for _ in range(4):
                split_lo()
            pre_norm("g_mix_pre")

            for c in range(16):
                step()
                if c == 5:
                    dve.wait_ge(S["evac"], EV_IN + 4)
                    n = 16 + SEQ
                    chained(dve.tensor_tensor(pad_b[:, :, 1:n], u_pad[:, :, 1:n], u_pad[:, :, 0:n - 1], ALU.add))
                    chained(dve.tensor_tensor(pad_c[:, 1:4, 2:n], pad_b[:, 1:4, 2:n], pad_b[:, 1:4, 0:n - 2], ALU.add))
                if c == 6:
                    chained(dve.tensor_tensor(pad_b[:, 2:4, 4:n], pad_c[:, 2:4, 4:n], pad_c[:, 2:4, 0:n - 4], ALU.add))
                    chained(dve.tensor_tensor(pad_c[:, 3, 8:n], pad_b[:, 3, 8:n], pad_b[:, 3, 0:n - 8], ALU.add))
                if c == 7:
                    sums = [pad_b, pad_c, pad_b, pad_c]
                    for g in range(4):
                        own.done(dve.scalar_tensor_tensor(proj[:, g, :], sums[g][:, g, 16:], 0.5 ** (g + 1),
                                                          u_pad[:, g, 16:], ALU.mult, ALU.subtract))
                    own.settle()
                    for g in range(4):
                        own.done(dve.tensor_tensor(proj[:, g, 0:16], sums[g][:, g, 16:32], invc[:, g, :], ALU.mult))
                    own.settle()
                    dve.tensor_tensor(proj[:, 0:4, 0:16], proj[:, 0:4, 0:16], u_pad[:, :, 16:32], ALU.subtract
                                      ).then_inc(S["pooled"], 1)
            dve.wait_ge(S["pool_mixed"], 1)
            for g in range(4):
                src = chunk(6 + g // 2, g % 2)
                chained(dve.tensor_scalar(mix_hi[:, g, :], src, vcol("pool_scale", g), None, ALU.mult))
                dve.scalar_tensor_tensor(mix_lo[:, g, :], src, vcol("pool_scale", g), fp(mix_hi[:, g, :]),
                                         ALU.mult, ALU.subtract).then_inc(S["mix_ready"], 1)
            dve.wait_ge(S["bias_copied"], HEADS)
            attention(HEADS, lambda h: bias[:, h, :], DH ** -0.5, [0, 1, 1, 1, 1, 1, 1, 0, 1, 1], 2)
            unit_done()
            post_norm("g_mix_post")
            pre_norm("g_ffn_pre")
            dve.wait_ge(S["p_hi_done"], 1)
            dve.tensor_tensor(p_lo, pt[:], fp(p_hi), ALU.subtract).then_inc(S["p_split"], 1)
            feed_forward(True)
            unit_done()
            post_norm("g_ffn_post")
            operand_lo(x)
            step()
            step()
            for c in range(NCH):
                step()
                dve.wait_ge(S["sig_done"], c + 1)
                chained(dve.tensor_tensor(sq[:, c, :], sq[:, c, :], acc(c), ALU.mult))
                m = dve.tensor_tensor(x[:, c, :], x[:, c, :], sq[:, c, :], ALU.add)
                if c % 2:
                    m.then_inc(S["x_ready"], 1)
            operand_lo(x)
            for c in range(18):
                step()
                if c == 13:
                    dve.wait_ge(S["evac"], EV_EVEN + 12)
                    z = proj[:, 4:8, :]
                    chained(dve.tensor_tensor(z, z, proj[:, 8:12, :], ALU.mult))
                if c == 14:
                    for tap in (2, 1, 0):
                        for g in range(4):
                            w = vcol("ev_conv_w", 4 * tap + g)
                            if tap == 2:
                                m = dve.tensor_scalar(sq[:, g, :], z[:, g, :], w, None, ALU.mult)
                            else:
                                a = 2 - tap
                                m = dve.scalar_tensor_tensor(sq[:, g, a:], z[:, g, 0:SEQ - a], w, sq[:, g, a:],
                                                             ALU.mult, ALU.add)
                            own.done(m)
                        own.settle()
                if c == 15:
                    chained(dve.tensor_tensor(sq[:, 0:4, :], sq[:, 0:4, :], proj[:, 0:4, :], ALU.mult))
                if c == 16:
                    put_mix(0, 4, sq[:, 0:4, :])
            attention(HEADS, lambda h: masks[:, 1, :], DH ** -0.5, [0, 1, 1, 1, 1, 1, 1, 0, 1, 1], 2,
                      sink=lambda h: h // 2 + 4 * (h % 2))
            unit_done()
            layer_norm("ln_mix_g", "ln_mix_b", 0)
            operand_lo(x)
            feed_forward(False)
            unit_done()
            layer_norm("ln_ffn_g", "ln_ffn_b", 0)
            operand_lo(x)
            def halves(t, m):
                v = t.rearrange("p (g r) -> p g r", r=2 * m)
                return v[:, :, 0:m], v[:, :, m:2 * m]

            def quarters(t):
                v = t.rearrange("p (a q r) -> p a q r", a=2, q=4)
                return [v[:, :, i, :] for i in range(4)]

            def differences(i, m):
                if i > 1:
                    dve.wait_ge(S["decay_exp"], i - 1)
                bl, br = halves(gb, min(m, 64))
                dl, dr = halves(gd, min(m, 64))
                ref = bl[:, :, m - 1:m].to_broadcast(list(bl.shape)) if m <= 64 else None
                if m < 64:
                    own.done(dve.tensor_tensor(dl, ref, bl, ALU.subtract))
                    dve.tensor_tensor(dr, br, ref, ALU.subtract).then_inc(S["decay_ready"], 1)
                elif m == 64:
                    own.done(dve.tensor_tensor(dl, ref, bl, ALU.subtract))
                    dve.tensor_copy(dr, br).then_inc(S["decay_ready"], 1)
                else:
                    b, dd = quarters(gb), quarters(gd)
                    own.done(dve.tensor_tensor(dd[0], dd[0], b[1][:, :, 63:64].to_broadcast(list(b[0].shape)), ALU.add))
                    own.done(dve.tensor_tensor(dd[1], b[1][:, :, 63:64].to_broadcast(list(b[0].shape)), b[1], ALU.subtract))
                    own.done(dve.tensor_copy(dd[2], b[2]))
                    dve.tensor_tensor(dd[3], b[3], b[2][:, :, 63:64].to_broadcast(list(b[0].shape)), ALU.add
                                      ).then_inc(S["decay_ready"], 1)

            def decayed(i, m):
                dve.wait_ge(S["decay_exp"], i)
                if i > 2:
                    dve.wait_ge(S["level_done"], i - 1)
                dst = gqk[:, i % 2 if m <= 64 else 0, :]
                (ol, orr), (el, er) = halves(dst, m), halves(ge, m)
                kl, _ = halves(proj[:, 6:8, :].rearrange("p a t -> p (a t)"), m)
                _, qr = halves(proj[:, 4:6, :].rearrange("p a t -> p (a t)"), m)
                own.done(dve.tensor_tensor(ol, el, kl, ALU.mult))
                dve.tensor_tensor(orr, er, qr, ALU.mult).then_inc(S["decayed"], 1)

            def keep(i):
                dve.wait_ge(S["level_done"], i + 1)
                mask = gmask[:, i, :].unsqueeze(1).to_broadcast([P, 4, P])
                for r in range(2):
                    m = dve.copy_predicated(att[:, r, :].rearrange("p (a k) -> p a k", a=4), mask,
                                            bank(6 + r).rearrange("p (a k) -> p a k", a=4))
                    if r == 0:
                        own.done(m)
                m.then_inc(S["level_kept"], 1)

            own.done(dve.memset(att, 0.0))
            for c in range(12):
                step()
                if c == 8:
                    dve.wait_ge(S["gate_z"], 1)
                    own.done(dve.tensor_scalar(gd[:, 0:SEQ], chunk(7, 0), vcol("b_gate", 0), None, ALU.add))
                    dve.tensor_scalar(gd[:, SEQ:512], chunk(7, 1), vcol("b_gate", 1), None, ALU.add
                                      ).then_inc(S["gate_zb"], 1)
                if c == 9:
                    dve.wait_ge(S["mla_root"], 1)
                    chained(dve.reciprocal(rinv[:], root[:]))
                    for j in range(2):
                        own.done(dve.scalar_tensor_tensor(y[:, j, :], proj[:, j, :], vcol("q_g", j), rinv[:, 0:SEQ],
                                                          ALU.mult, ALU.mult))
                    dve.scalar_tensor_tensor(y[:, 2, :], proj[:, 3, :], vcol("kv_g", 0), rinv[:, SEQ:512],
                                             ALU.mult, ALU.mult).then_inc(S["mla_normed"], 1)
                    dve.wait_ge(S["softplus_done"], 1)
                    chained(dve.scalar_tensor_tensor(gd, gd, 0.0, ge, ALU.min, ALU.subtract))
                    own.done(dve.tensor_tensor_scan(gb[:, 0:SEQ], scan0[:], gd[:, 0:SEQ], 0.0, ALU.mult, ALU.add))
                    chained(dve.tensor_tensor_scan(gb[:, SEQ:512], scan0[:], gd[:, SEQ:512], 0.0, ALU.mult, ALU.add))
                    differences(1, 1)
                if c == 10:
                    keep(0)
                if c == 11:
                    dve.wait_ge(S["mla_hi"], 1)
                    dve.tensor_tensor(mix_lo[:, 4:7, :], y[:, 0:3, :], fp(mix_hi[:, 4:7, :]), ALU.subtract
                                      ).then_inc(S["mla_split"], 1)
                    decayed(1, 1)
                    differences(2, LEVELS[2])
            for i in range(4):
                step()
                decayed(2 + i, LEVELS[2 + i])
                keep(1 + i)
                differences(3 + i, LEVELS[3 + i])
            step()
            lo_q, hi_q = slice(64, 96), slice(96, 128)
            cos, sin = rope[lo_q, :], rope[hi_q, :]
            turned = sq[lo_q, 4:8, :]
            unit_done()
            for b in range(2):
                own.done(dve.tensor_tensor(mq[lo_q, 2 * b:2 * b + 2, :],
                                           ps[lo_q, b, :].rearrange("p (c t) -> p c t", c=2), over(cos, 2), ALU.mult))
                own.done(dve.tensor_tensor(turned[:, 2 * b:2 * b + 2, :],
                                           ps[hi_q, b, :].rearrange("p (c t) -> p c t", c=2), over(sin, 2), ALU.mult))
            own.settle()
            chained(dve.tensor_tensor(mq[lo_q, :, :], mq[lo_q, :, :], turned, ALU.add))
            own.done(dve.tensor_tensor(turned[:, 0, :], proj[lo_q, 2, :], cos, ALU.mult))
            chained(dve.tensor_tensor(turned[:, 1, :], proj[hi_q, 2, :], sin, ALU.mult))
            chained(dve.tensor_tensor(turned[:, 2, :], turned[:, 0, :], turned[:, 1, :], ALU.add))
            own.done(dve.tensor_copy(mk[lo_q, :, :], over(turned[:, 2, :], 4)))
            step()
            decayed(6, LEVELS[6])
            keep(5)
            differences(7, LEVELS[7])
            decayed(7, LEVELS[7])
            keep(6)
            differences(8, 128)
            decayed(8, 128)
            keep(7)
            dve.wait_ge(S["level_done"], 9)
            own.done(dve.tensor_copy(cross[:, 0, :], bank(6, 0, SEQ)))
            dve.tensor_copy(cross[:, 1, :], bank(7, 0, SEQ)).then_inc(S["cross_kept"], 1)
            dve.wait_ge(S["mla_evac"], 3)
            own.settle()
            dve.wait_ge(S["cross_kept"], 1)
            dve.sem_inc(S["rope_done"], 1)
            for a in range(2):
                dve.wait_ge(S["gla_root"], a + 1)
                chained(dve.reciprocal(rinv[:], root[:]))
                o = pair(sq, a)
                chained(dve.scalar_tensor_tensor(o, bank2(6 + a), vcol("gla_g", 0), rinv[:].rearrange("p (c t) -> p c t", c=2),
                                                 ALU.mult, ALU.mult))
                chained(dve.tensor_tensor(o, o, proj[:, 8 + 2 * a:10 + 2 * a, :], ALU.mult))
                put_mix(2 * a, 2, o)
            attention(MLA_H, lambda h: masks[:, 0, :], MLA_QK ** -0.5, [0, 1, 1, 1, 1, 4], 1)
            unit_done()
            layer_norm("ln_mix_g", "ln_mix_b", 1)
            operand_lo(x)
            feed_forward(False, late=2)
            unit_done()
            layer_norm("ln_ffn_g", "ln_ffn_b", 1)
            assert unit.n == UNITS and split.n == UNITS, (unit.n, split.n)


def units_of(w, per_chunk):
    k, n = w.shape
    t = w.reshape(k // P, P, n // P, P)
    if per_chunk == "out":
        return t.transpose(2, 1, 0, 3).reshape(n // P, P, k)
    return t.transpose(0, 1, 2, 3).reshape(k // P, P, n)


def token_units(w):
    k, n = w.shape
    per = UNIT // n
    return w.reshape(k // P // per, per, P, n).transpose(0, 2, 1, 3).reshape(-1, P, UNIT)


def feed_forward_units(w_gate, w_up, w_down):
    g, u, dn = units_of(w_gate, "out"), units_of(w_up, "out"), units_of(w_down, "in")
    order = [g[0], u[0], g[1], u[1]]
    for j in range(2, NFF):
        order += [dn[j - 2], g[j], u[j]]
    return np.stack(order + [dn[NFF - 2], dn[NFF - 1]])


def stream_of(i):
    zero = lambda k, n: np.zeros((k, n), np.float32)
    w = i["w_in"][0]
    parts = [units_of(w[:, 0:1536], "out"), token_units(w[:, 1536:]), units_of(i["w_out"][0], "in"),
             feed_forward_units(i["w_up"][0][:, :D_FF], i["w_up"][0][:, D_FF:], i["w_down"][0]),
             units_of(i["w_ple"][0], "in"), units_of(i["w_ple_gate"][0], "out")]
    pairs = np.concatenate([np.arange(h * 64, h * 64 + 64) for c in range(4) for h in (c, 4 + c)])
    w = i["ev_w_in_2"][0]
    parts += [units_of(np.concatenate([w[:, 0:1536], w[:, 1536:2048][:, pairs], w[:, 2048:2176]], 1), "out"),
              token_units(w[:, 2176:]),
              units_of(i["ev_w_out_2"][0][np.concatenate([np.arange(512), 512 + pairs])], "in"),
              feed_forward_units(i["ffn_w_gate_2"][0], i["ffn_w_up_2"][0], i["ffn_w_down_2"][0])]
    w = i["od_w_in_2"][0]
    gq, gk, gv, low, gr, cq, ckv, kr = np.split(w, np.cumsum([256, 256, 512, 16, 512, 256, 128])[:7], axis=1)
    turned = lambda t: np.concatenate([t[:, 16:], t[:, :16]], 1)
    misc = np.concatenate([low, zero(D, 48), kr, turned(kr)], 1)
    parts += [units_of(np.concatenate([cq, misc, ckv, gq, gk, gr], 1), "out"), token_units(gv)]
    uq, ukv = i["od_mla_w_uq_2"][0], i["od_mla_w_ukv_2"][0]
    q = [np.concatenate([uq[:, h * 96:h * 96 + 96], turned(uq[:, h * 96 + 64:h * 96 + 96])], 1) for h in range(MLA_H)]
    q = np.concatenate(q, 1)
    kk = [np.concatenate([ukv[:, h * 192:h * 192 + 64], zero(P, 64)], 1) for h in range(MLA_H)]
    vv = [ukv[:, h * 192 + 64:h * 192 + 192] for h in range(MLA_H)]
    parts += [np.concatenate([q[:P], q[P:]], 1)[None], np.concatenate(kk + vv, 1)[None],
              units_of(i["od_w_out_2"][0], "in"),
              feed_forward_units(i["ffn_w_gate_2"][1], i["ffn_w_up_2"][1], i["ffn_w_down_2"][1])]
    return np.ascontiguousarray(np.concatenate(parts, 0))


def columns(v):
    return v.reshape(-1, P).T


def vectors_of(i):
    gla = i["od_gla_norm_g_2"][0]
    parts = [columns(i[n][0]) for n in ("g_mix_pre", "g_mix_post", "g_ffn_pre", "g_ffn_post", "pool_scale")]
    parts += [columns(i["conv_w"][0].reshape(-1)), columns(i["conv_b"][0]), columns(i["ev_conv_w_2"][0].reshape(-1))]
    parts += [columns(i[n].reshape(-1)) for n in ("ln_mix_g_2", "ln_mix_b_2", "ln_ffn_g_2", "ln_ffn_b_2",
                                                  "od_gla_b_gate_2", "od_gla_norm_g_2", "od_mla_q_norm_g_2",
                                                  "od_mla_kv_norm_g_2")]
    parts.append(np.tile(i["ev_sinks_2"].reshape(1, 8), (P, 1)))
    return np.ascontiguousarray(np.concatenate(parts, 1))


def constants():
    dist = 255 - np.arange(384)
    n = np.maximum(dist, 0)
    nf = np.maximum(n, 1).astype(np.float32)
    half = BUCKETS // 2
    large = half + (np.log(nf / np.float32(half)) / np.float32(math.log(MAX_DISTANCE / half)) * half).astype(np.int32)
    bucket = np.where(n < half, n, np.minimum(large, BUCKETS - 1))
    strip = np.zeros((BUCKETS + 1, 384), np.float32)
    strip[bucket, np.arange(384)] = dist >= 0
    strip[BUCKETS] = np.where(dist >= 0, 0.0, NEG)
    tok = np.arange(P)
    diag = np.where(tok[:, None] >= tok, 0.0, NEG)
    causal = np.concatenate([diag, np.zeros((P, P)), diag], 1)
    window = np.concatenate([diag, np.where(tok[:, None] < tok, 0.0, NEG), diag], 1)
    invc = np.stack([1.0 / np.minimum(np.arange(16) + 1, 2 ** (g + 1)) for g in range(4)])
    s, t = tok[:, None], tok[None, :]
    gmask = [(s == t)] + [(s // (2 * m) == t // (2 * m)) & (s % (2 * m) < m) & (t % (2 * m) >= m) for m in LEVELS[1:]]
    inv = np.float32(10000.0) ** (-np.arange(0, 32, 2, dtype=np.float32) / np.float32(32))
    ang = np.arange(SEQ, dtype=np.float32)[None, :] * inv.astype(np.float32)[:, None]
    cos, sin = np.cos(ang), np.sin(ang)
    rope = np.zeros((P, SEQ))
    rope[64:96] = np.concatenate([cos, cos])
    rope[96:128] = np.concatenate([-sin, sin])
    return {"strip": strip.reshape(BUCKETS + 1, 2, 192), "flip": np.eye(P)[::-1], "ident": np.eye(P),
            "invc": np.tile(invc[None], (P, 1, 1)), "masks": np.stack([causal, window], 1), "rope": rope,
            "gmask": np.stack(gmask, 1),
            "scan0": np.tile(((np.arange(SEQ) % GLA_CHUNK) != 0)[None], (P, 1))}


def features(v):
    return np.ascontiguousarray(v.T.reshape(-1, P, SEQ).transpose(1, 0, 2))


def arrays_of(i):
    a = {k: np.ascontiguousarray(v.astype(np.float32)) for k, v in constants().items()}
    a["stream"] = stream_of(i)
    a["x"] = features(i["x"][0])
    a["p"] = features(i["p"][0, 0])
    a["vec"] = vectors_of(i)
    a["rel"] = np.concatenate([i["rel_bias"], np.ones((1, HEADS), np.float32)], 0)
    a["wpool"] = np.ascontiguousarray(i["w_pool"][0].transpose(1, 0, 2))
    a["w_gate"] = i["od_gla_w_gate_2"][0]
    return a


def kernel(**inputs):
    import concourse.bacc as bacc
    from concourse.bass_utils import run_bass_kernel_spmd as run

    nc = bacc.Bacc("TRN2", target_bir_lowering=False, num_devices=1)
    arrays = arrays_of({k: np.asarray(v) for k, v in inputs.items()})
    d = {n: nc.dram_tensor(f"in_{n}", a.shape, mybir.dt.from_np(a.dtype), kind="ExternalInput").ap()
         for n, a in arrays.items()}
    out = nc.dram_tensor("result", (P, NCH, SEQ), F32, kind="ExternalOutput").ap()
    build(nc, d, out)
    r = run(nc, [{f"in_{n}": a for n, a in arrays.items()}], core_ids=[0])
    got = r.results[0]["result"]
    return np.ascontiguousarray(got.transpose(2, 1, 0).reshape(1, SEQ, D))
```

```python
from contextlib import ExitStack
import math

import numpy as np

import concourse.bass as bass
from concourse import mybir

F32 = mybir.dt.float32
F32R = mybir.dt.float32r
U8 = mybir.dt.uint8
ALU = mybir.AluOpType
ACT = mybir.ActivationFunctionType
AX_X = mybir.AxisListType.X

P = 128
SEQ = 256
D = 1024
NCH = D // P
PLE = 256
HEADS, DH = 8, 64
D_FF = 2816
NFF = D_FF // P
ALPHA = 4.0 ** 0.25
RMS_EPS, LN_EPS = 1e-6, 1e-5
BUCKETS, MAX_DISTANCE = 32, 128
GLA_H, GLA_CHUNK, GLA_TAU = 4, 64, 16.0
MLA_H, MLA_QK = 4, 96
NEG = -1e30
UNIT = 1024
SLOTS = 6

U_IN = 0
U_OUT = U_IN + 16
U_FFN1 = U_OUT + 8
U_PLE = U_FFN1 + 3 * NFF
U_EV_IN = U_PLE + 10
U_EV_OUT = U_EV_IN + 18
U_FFN2 = U_EV_OUT + 8
U_OD_IN = U_FFN2 + 3 * NFF
U_MLA = U_OD_IN + 16
U_OD_OUT = U_MLA + 2
U_FFN3 = U_OD_OUT + 8
UNITS = U_FFN3 + 3 * NFF

VEC, _at = {}, 0
for _name, _n in (("g_mix_pre", 8), ("g_mix_post", 8), ("g_ffn_pre", 8), ("g_ffn_post", 8),
                  ("pool_scale", 4), ("conv_w", 3 * NFF), ("conv_b", NFF), ("ev_conv_w", 12),
                  ("ln_mix_g", 16), ("ln_mix_b", 16), ("ln_ffn_g", 16), ("ln_ffn_b", 16),
                  ("b_gate", 2), ("gla_g", 1), ("q_g", 2), ("kv_g", 1), ("sinks", 8)):
    VEC[_name] = _at
    _at += _n
N_VEC = _at
LEVELS = (0, 1, 2, 4, 8, 16, 32, 64)


class Cursor:

    def __init__(self):
        self.n, self.turn, self.per = 0, None, 0

    def at(self, more=0):
        n = self.n + more
        return n if self.turn is None else self.turn * self.per + n

    def enter(self, turn, per):
        self.turn, self.per, self.start = turn, per, self.n

    def leave(self, turns):
        assert self.n - self.start == self.per, (self.n, self.start, self.per)
        self.n, self.turn = self.start + self.per * turns, None


class Chain:

    def __init__(self, eng, sem):
        self.eng, self.sem, self.count = eng, sem, Cursor()

    def done(self, ins):
        self.count.n += 1
        return ins.then_inc(self.sem, 1)

    def settle(self):
        self.eng.wait_ge(self.sem, self.count.at())


def build(nc, d, out):
    with ExitStack() as ctx:
        def sb(name, shape, dt=F32):
            return ctx.enter_context(nc.sbuf_tensor(name, shape, dt))

        def sem(name):
            return ctx.enter_context(nc.semaphore(name))

        raw = sb("raw", [P, SLOTS, UNIT])
        w_hi = sb("w_hi", [P, SLOTS, UNIT], F32R)
        w_lo = sb("w_lo", [P, SLOTS, UNIT], F32R)
        x = sb("x", [P, NCH, SEQ])
        op_hi = sb("op_hi", [P, NCH, SEQ], F32R)
        op_lo = sb("op_lo", [P, NCH, SEQ], F32R)
        mix_hi = sb("mix_hi", [P, NCH, SEQ], F32R)
        mix_lo = sb("mix_lo", [P, NCH, SEQ], F32R)
        y = sb("y", [P, NCH, SEQ])
        sq = sb("sq", [P, NCH, SEQ])
        proj = sb("proj", [P, 16, SEQ])
        vtok = sb("vtok", [P, 2, 512])
        rinv = sb("rinv", [P, 512])
        tok_var = sb("tok_var", [P, 8])
        tok_rinv = sb("tok_rinv", [P, 8])
        tok_ffn = sb("tok_ffn", [P, 2])
        first = sb("first", [P, 1])
        minus_half = sb("minus_half", [P, 8])
        bias = sb("bias", [P, HEADS, 384])
        logit = sb("logit", [P, 2, 384])
        probT = sb("probT", [P, 2, 384])
        stat = sb("stat", [P, 2, 8])
        work = sb("work", [P, 17, SEQ])
        vec = sb("vec", [P, N_VEC])
        ident = sb("ident", [P, P])
        flip = sb("flip", [P, P])
        mean_w = sb("mean_w", [P, 3, P])
        wpool = sb("wpool", [P, 4, P])
        w_gate = sb("w_gate", [16, 256])
        rel = sb("rel", [BUCKETS + 1, HEADS])
        invc = sb("invc", [P, 4, 16])
        masks = sb("masks", [P, 2, 384])
        rope = sb("rope", [P, SEQ])
        gmask = sb("gmask", [P, len(LEVELS), P], U8)
        scan0 = sb("scan0", [P, SEQ])
        pt = sb("pt", [P, 2, SEQ])
        ps = ctx.enter_context(nc.psum_tensor("ps", [P, 8, 512], F32))
        scratch = nc.dram_tensor("bias_rows", (HEADS, 384), F32, kind="Internal")

        gmask_f = proj[:, 12:16, :].rearrange("p a b -> p (a b)").rearrange("p (l k) -> p l k", l=len(LEVELS))
        skew = y
        strip = work[0:BUCKETS + 1, 15:17, 0:192]
        table = work[0:HEADS, 13:15, 0:192]
        pads = work[:, 0:13, :].rearrange("p a b -> p (a b)")[:, 0:12 * (16 + SEQ)] \
            .rearrange("p (k c t) -> p k c t", k=3, c=4)
        u_pad, pad_b, pad_c = pads[:, 0], pads[:, 1], pads[:, 2]
        h_hi, h_lo = mix_hi[:, 0:2, :], mix_lo[:, 0:2, :]
        p_hi, p_lo = mix_hi[:, 2:4, :], mix_lo[:, 2:4, :]
        h_fp, gate, conv, gate_n = (proj[:, i:i + 2, :] for i in (0, 2, 4, 6))
        flat = work[:, :, :].rearrange("p a b -> p (a b)")
        att = flat[:, 0:1024].rearrange("p (a b) -> p a b", a=2)
        gb, gd, ge = flat[:, 1024:1536], flat[:, 1536:2048], flat[:, 2048:2560]
        gdd = proj[:, 12:16, :].rearrange("p (a c) t -> p a (c t)", a=2)
        gee = flat[:, 1536:2560].rearrange("p (a b) -> p a b", a=2)
        gk = flat[:, 2560:3584].rearrange("p (i b) -> p i b", i=2)
        gq = [v.rearrange("p b (h k) -> p b h k", h=2) for v in (sq[:, 0:4, :], y[:, 4:8, :])]
        cross = flat[:, 3584:4096].rearrange("p (a b) -> p a b", a=2)
        wide = bias[:, :, :].rearrange("p a b -> p (a b)")
        mq = wide[:, 0:1024].rearrange("p (h t) -> p h t", h=4)
        mk = wide[:, 1024:2048].rearrange("p (h t) -> p h t", h=4)
        mv = wide[:, 2048:3072].rearrange("p (t n) -> p t n", t=2)
        swa_k = y[:, 0, :]
        gla_o = proj[:, 12:16, :].rearrange("p (a c) t -> p a (c t)", a=2)

        names = """vec_loaded consts_loaded late_loaded pool_const table_ready table_copied table_stored skew_loaded
            flip_done bias_copied split_hi_done split_done units_done sq_ready sq_summed mean_done
            stat_done var_ready tok_rinv_ready spread_done x_ready norm_hi operand_ready acc_free z_ready centred evac
            pooled pool_mixed mix_ready scores_done logits_done shift_ready probs_done probs_scaled
            probT_done probT_copied heads_done conv_done gate_act h_ready scaled
            p_hi_done p_split sig_done gate_z gate_zb softplus_done decay_ready decay_exp decayed
            level_done level_kept cross_kept gla_out gla_sq gla_copied
            mla_sq mla_normed rinv_ready mla_hi mla_split rope_done mla_evac
            act_step dve_step result_ready acc_done pool_step gate_summed rinv_copied out_stored""".split()
        S = {n: sem(n) for n in names}
        raw_loaded = [sem(f"raw_loaded_{s}") for s in range(SLOTS)]
        EV_IN, EV_EVEN, EV_ODD = 0, 14, 14 + 19
        x_loaded = [sem(f"x_loaded_{i}") for i in range(4)]
        level_bank = (0, 2, 6, 0, 2, 6, 6, 0)
        STATISTICS = (2, 2, 2, 2, 2, 2, 4, 8, 2, 2)

        def bank(b, a=0, n=512):
            return ps[:, b, a:a + n]

        def chunk(b, c):
            return ps[:, b, c * SEQ:c * SEQ + SEQ]

        def acc(c):
            return chunk(c // 2, c % 2)

        def pair(t, i):
            return t[:, 2 * i:2 * i + 2, :]

        def bank2(b):
            return ps[:, b, :].rearrange("p (c t) -> p c t", c=2)

        def vcol(name, c, n=1):
            at = VEC[name] + c
            return vec[:, at:at + n]

        def fp(ap):
            return ap.bitcast(F32)

        def over(ap, n):
            return ap.unsqueeze(1).to_broadcast([ap.shape[0], n, ap.shape[1]])

        def halves(t, m):
            v = t.rearrange("p (g r) -> p g r", r=2 * m)
            return v[:, :, 0:m], v[:, :, m:2 * m]

        def quarters(t):
            v = t.rearrange("p (a q r) -> p a q r", a=2, q=4)
            return [v[:, :, i, :] for i in range(4)]

        block = ctx.enter_context(nc.Block())

        @block.sync
        def _(sp):
            sp.dma_start(vec[:], d["vec"]).then_inc(S["vec_loaded"], 16)
            sp.dma_start(pair(x, 0), pair(d["x"], 0)).then_inc(x_loaded[0], 16)
            sp.dma_start(raw[:, 0, :], d["stream"][0]).then_inc(raw_loaded[0], 16)
            for i in range(1, 4):
                sp.dma_start(pair(x, i), pair(d["x"], i)).then_inc(x_loaded[i], 16)
            for s in range(1, SLOTS):
                sp.dma_start(raw[:, s, :], d["stream"][s]).then_inc(raw_loaded[s], 16)
            rounds = UNITS // SLOTS
            with sp.Fori(1, rounds) as r:
                at = [sp.snap(r * SLOTS + s) for s in range(SLOTS)]
                for s in range(SLOTS):
                    sp.wait_ge(S["split_done"], r * SLOTS + (s - SLOTS + 1))
                    sp.dma_start(raw[:, s, :], d["stream"][bass.ds(at[s], 1)].rearrange("a p n -> p (a n)")
                                 ).then_inc(raw_loaded[s], 16)
            for v in range(rounds * SLOTS, UNITS):
                sp.wait_ge(S["split_done"], v - SLOTS + 1)
                sp.dma_start(raw[:, v % SLOTS, :], d["stream"][v]).then_inc(raw_loaded[v % SLOTS], 16)
            for i in range(4):
                sp.wait_ge(S["result_ready"], i + 1)
                sp.dma_start(pair(out, i), pair(x, i)).then_inc(S["out_stored"], 16)
            sp.wait_ge(S["out_stored"], 64)

        consts = [("rel", rel[:]), ("strip", strip), ("ident", ident[:]), ("flip", flip[:]), ("invc", invc[:])]
        late_consts = [("wpool", wpool[:]), ("masks", masks[:]), ("p", pt[:]), ("rope", rope[:]), ("gmask", gmask_f),
                       ("scan0", scan0[:]), ("w_gate", w_gate[:])]

        @block.gpsimd
        def _(pool):
            def inverse_root(i):
                n = STATISTICS[i]
                pool.wait_ge(S["var_ready"], i + 1)
                m = pool.tensor_tensor(tok_rinv[:, 0:n], tok_var[:, 0:n], minus_half[:, 0:n], ALU.pow)
                if i == 2:
                    m.then_inc(S["pool_step"], 1)
                    pool.wait_ge(S["pool_step"], 1)
                    m = pool.tensor_copy(tok_ffn[:], tok_rinv[:, 0:2])
                if i == 3:
                    m.then_inc(S["pool_step"], 1)
                    pool.wait_ge(S["pool_step"], 2)
                    m = pool.tensor_tensor(tok_rinv[:, 0:2], tok_rinv[:, 0:2], tok_ffn[:], ALU.mult)
                m.then_inc(S["tok_rinv_ready"], 1)

            pool.memset(mean_w[:, 0, :], 1.0 / D).then_inc(S["pool_const"], 1)
            pool.memset(mean_w[:, 1, :], 1.0 / 256).then_inc(S["pool_const"], 1)
            pool.memset(mean_w[:, 2, :], 1.0 / 128).then_inc(S["pool_const"], 1)
            pool.memset(minus_half[:], -0.5).then_inc(S["pool_const"], 1)
            pool.memset(pad_b[:, :, 0:16], 0.0).then_inc(S["pool_const"], 1)
            pool.memset(pad_c[:, :, 0:16], 0.0).then_inc(S["pool_const"], 1)
            pool.memset(u_pad[:, :, 0:16], 0.0).then_inc(S["pool_const"], 1)
            inverse_root(0)
            pool.wait_ge(S["table_copied"], 1)
            pool.dma_start(scratch.ap().rearrange("h (a b) -> h a b", a=2), table).then_inc(S["table_stored"], 16)
            pool.wait_ge(S["table_stored"], 16)
            pool.dma_start(skew[:], bass.AP(scratch, 0, [[1, P], [384, HEADS], [1, SEQ]])
                           ).then_inc(S["skew_loaded"], 16)
            pool.wait_ge(S["late_loaded"], 16 * len(late_consts))
            pool.tensor_copy(gmask[:], gmask_f).then_inc(S["pool_const"], 1)
            for i in range(1, 6):
                inverse_root(i)
            pool.memset(gk, 0.0).then_inc(S["pool_step"], 1)
            pool.wait_ge(S["gate_zb"], 1)
            pool.memset(gq[0], 0.0).then_inc(S["pool_step"], 1)
            pool.memset(gq[1], 0.0).then_inc(S["pool_step"], 1)

            pool.wait_ge(S["gate_summed"], 1)
            for i in range(1, 9):
                if i > 2:
                    pool.wait_ge(S["decay_exp"], i - 2)
                m, g = LEVELS[min(i, 7)], gdd[:, i % 2, :]
                bl, br = halves(gb, m)
                dl, dr = halves(g, m)
                ref = bl[:, :, m - 1:m].to_broadcast(list(bl.shape))
                b, dd = quarters(gb), quarters(g)
                if i < 7:
                    pool.tensor_tensor(dl, ref, bl, ALU.subtract).then_inc(S["pool_step"], 1)
                    pool.tensor_tensor(dr, br, ref, ALU.subtract).then_inc(S["decay_ready"], 1)
                elif i == 7:
                    pool.tensor_tensor(dl, ref, bl, ALU.subtract).then_inc(S["pool_step"], 1)
                    pool.tensor_copy(dr, br).then_inc(S["decay_ready"], 1)
                else:
                    pool.tensor_tensor(dd[0], b[0][:, :, 63:64].to_broadcast(list(b[0].shape)), b[0], ALU.subtract
                                       ).then_inc(S["pool_step"], 1)
                    pool.wait_ge(S["pool_step"], 5 + 8)
                    pool.tensor_tensor(dd[0], dd[0], b[1][:, :, 63:64].to_broadcast(list(b[0].shape)), ALU.add
                                       ).then_inc(S["pool_step"], 1)
                    pool.tensor_tensor(dd[1], b[1][:, :, 63:64].to_broadcast(list(b[0].shape)), b[1], ALU.subtract
                                       ).then_inc(S["pool_step"], 1)
                    pool.tensor_copy(dd[2], b[2]).then_inc(S["pool_step"], 1)
                    pool.tensor_tensor(dd[3], b[3], b[2][:, :, 63:64].to_broadcast(list(b[0].shape)), ALU.add
                                       ).then_inc(S["decay_ready"], 1)
                if i == 2:
                    inverse_root(6)
            for i in range(7, len(STATISTICS)):
                inverse_root(i)

        @block.tensor
        def _(pe):
            unit, sq_count, hidden, head_count = Cursor(), Cursor(), Cursor(), Cursor()

            def take():
                pe.wait_ge(S["split_done"], unit.at(1))
                return unit.n % SLOTS

            def given(last):
                last.then_inc(S["units_done"], 1)
                unit.n += 1

            def three(o, wh, wl, xh, xl, start, stop, **kw):
                pe.matmul(o, wh, xh, start=start, stop=False, **kw)
                pe.matmul(o, wh, xl, start=False, stop=False, **kw)
                return pe.matmul(o, wl, xh, start=False, stop=stop, **kw)

            def first_chunks(o, p, operand):
                slots = (unit.n % SLOTS, (unit.n + 1) % SLOTS)
                for part in (((0,), (1,)) if operand == 0 else ((0, 1),)):
                    pe.wait_ge(S["split_done"], unit.at(part[-1] + 1))
                    for k in range(NCH):
                        if k % 2 == 0:
                            pe.wait_ge(S["norm_hi"], 4 * operand + k // 2 + 1)
                        w = slice(k * P, k * P + P)
                        for i in part:
                            s, dst = slots[i], (o, p)[i]
                            pe.matmul(dst, w_hi[:, s, w], op_hi[:, k, :], start=k == 0, stop=False)
                            pe.matmul(dst, w_lo[:, s, w], op_hi[:, k, :], start=False, stop=False)
                for k in range(NCH):
                    if k % 2 == 0:
                        pe.wait_ge(S["operand_ready"], 4 * operand + k // 2 + 1)
                    w = slice(k * P, k * P + P)
                    m = [pe.matmul(dst, w_hi[:, s, w], op_lo[:, k, :], start=False, stop=k == NCH - 1)
                         for dst, s in zip((o, p), slots)]
                for last in m:
                    given(last)

            def out_chunk(o):
                s = take()
                for k in range(NCH):
                    w = slice(k * P, k * P + P)
                    m = three(o, w_hi[:, s, w], w_lo[:, s, w], op_hi[:, k, :], op_lo[:, k, :], k == 0, k == NCH - 1)
                given(m)

            def in_chunk(xh, xl, first, last, by_bank=True, half=None):
                s = take()
                for c in range(NCH) if half is None else range(4 * half, 4 * half + 4):
                    w = slice(c * P, c * P + P)
                    m = three(acc(c), w_hi[:, s, w], w_lo[:, s, w], xh, xl, first and c % 2 == 0, last,
                              skip_group_check=True)
                    if last and by_bank and c in (1, 3, 5):
                        m.then_inc(S["acc_done"], 1)
                if half != 0:
                    given(m)

            def token_unit(n, xh, xl, k0, kn, last, s=None, col=0, banks=(4, 5)):
                s = take()
                for k in range(kn):
                    w = slice(k * n, k * n + n)
                    for t in range(2):
                        tok = slice(t * P, t * P + P)
                        o = bank(banks[t], 0, n)
                        a, b = xh[:, k0 + k, tok], xl[:, k0 + k, tok]
                        pe.matmul(o, a, w_hi[:, s, w], start=k0 + k == 0, stop=False)
                        pe.matmul(o, a, w_lo[:, s, w], start=False, stop=False)
                        m = pe.matmul(o, b, w_hi[:, s, w], start=False, stop=last and k == kn - 1)
                given(m)

            def mean_over_features(b, src):
                for piece in range(1, 4):
                    z_seen[0] += 1
                    pe.wait_ge(S["z_ready"], z_seen[0])
                    for c in (2 * piece, 2 * piece + 1):
                        z = sq[:, c - 2, :] if piece == 1 else src[:, c, :]
                        m = pe.matmul(chunk(b, 0), mean_w[:, 0, :], z, start=c == 2, stop=c == NCH - 1)
                m.then_inc(S["mean_done"], 1)
            z_seen = [0]

            def token_means(b, cols):
                parts = [(col, w, src) for col, w, chunks in cols for src in chunks]
                for i, (col, w, src) in enumerate(parts):
                    src = src() if callable(src) else src
                    for t in range(2):
                        m = pe.matmul(ps[:, b, col + t:col + t + 1], src[:, t * P:t * P + P], mean_w[:, w, 0:1],
                                      start=i + t == 0, stop=i + 1 == len(parts), skip_group_check=True)
                m.then_inc(S["stat_done"], 1)

            def square_mean(b):
                def src(c):
                    if c % 4 == 0:
                        sums[0] += 1
                        pe.wait_ge(S["sq_summed"], sums[0])
                    return sq[:, c, :]
                token_means(b, [(0, 0, [lambda c=c: src(c) for c in (0, 1, 4)])])
            sums = [0]

            def spread(places):
                spreads[0] += 1
                pe.wait_ge(S["tok_rinv_ready"], spreads[0])
                for i, (col, b, at) in enumerate(places):
                    m = pe.matmul(bank(b, at, P), tok_rinv[:, col:col + 1].to_broadcast([P, P]), ident[:],
                                  start=True, stop=True)
                m.then_inc(S["spread_done"], 1)
            spreads = [0]

            def mean_square(b):
                square_mean(b)
                spread([(0, b, SEQ), (1, b, SEQ + P)])

            def feed_forward(operand, norm=False):
                def up(c):
                    out_chunk(chunk(4 + 2 * c, 0))
                    out_chunk(chunk(5 + 2 * c, 0))

                def down(c, j, first=False, last=False):
                    pe.wait_ge(S["h_ready"], j)
                    in_chunk(h_hi[:, c, :], h_lo[:, c, :], first, last)

                j = hidden.n
                first_chunks(chunk(4, 0), chunk(5, 0), operand)
                if norm:
                    pe.wait_ge(S["acc_free"], 1)
                    square_mean(0)
                    out_chunk(chunk(6, 0))
                    spread([(0, 0, SEQ), (1, 0, SEQ + P)])
                    out_chunk(chunk(7, 0))
                    pe.wait_ge(S["rinv_copied"], 1)
                else:
                    up(1)
                down(0, j + 1, first=True)
                up(0)
                down(1, j + 2)
                up(1)
                turns = NFF // 2 - 2
                with pe.Fori(0, turns) as i:
                    unit.enter(i, 6)
                    down(0, i * 2 + (j + 3))
                    up(0)
                    down(1, i * 2 + (j + 4))
                    up(1)
                    unit.leave(turns)
                down(0, j + NFF - 1)
                down(1, j + NFF, last=True)
                hidden.n += NFF

            def attention(n, q, k, v, o, fillers, mixed, between={}):
                h0 = head_count.n
                fillers = [[c if isinstance(c, tuple) else (c, None) for c in f] for f in fillers]
                order = [c for f in fillers for c, _ in f]

                def filler(c, half):
                    pe.wait_ge(S["mix_ready"], mixed(c))
                    in_chunk(mix_hi[:, c, :], mix_lo[:, c, :], c == order[0], c == order[-1], half=half)

                def scores(h):
                    g, b = h0 + h, 4 + (h0 + h) % 2
                    if g >= 2:
                        pe.wait_ge(S["logits_done"], g - 1)
                    pe.matmul(bank(b, 0, P), q(h)[:, 0:P], k(h)[:, 0:P], start=True, stop=True)
                    pe.matmul(bank(b, P, SEQ), q(h)[:, P:SEQ], k(h), start=True, stop=True
                              ).then_inc(S["scores_done"], 1)

                def turn(h):
                    g = h0 + h
                    pe.wait_ge(S["probs_scaled"], g + 1)
                    if g:
                        pe.wait_ge(S["probT_copied"], g)
                    for j in range(3):
                        m = pe.transpose(bank(6, j * P, P), logit[:, g % 2, j * P:j * P + P], ident[:])
                    m.then_inc(S["probT_done"], 1)

                def values(h):
                    g = h0 + h
                    lo, free = o(h)
                    pe.wait_ge(S["probT_copied"], g + 1)
                    if free is not None:
                        pe.wait_ge(S["mix_ready"], free)
                    pe.matmul(ps[lo:lo + v(h, 0).shape[1], 7, 0:SEQ], v(h, 0), probT[:, g % 2, 0:SEQ],
                              start=True, stop=False, skip_group_check=True)
                    pe.matmul(ps[lo:lo + v(h, 0).shape[1], 7, P:SEQ], v(h, 1), probT[:, g % 2, SEQ:384],
                              start=False, stop=True, skip_group_check=True).then_inc(S["heads_done"], 1)

                for t in range(n + 2):
                    if t < n:
                        scores(t)
                    if t >= 2:
                        values(t - 2)
                    if t in between:
                        between[t]()
                    last = fillers[t][1:] if t == n else []
                    for f in fillers[t][:1] if t == n else fillers[t]:
                        filler(*f)
                    if 1 <= t <= n:
                        turn(t - 1)
                    for f in last:
                        filler(*f)
                head_count.n += n

            def bias_tile(h):
                if h >= 4:
                    pe.wait_ge(S["bias_copied"], h - 3)
                else:
                    pe.wait_ge(S["evac"], EV_IN + 9 + h)
                pe.matmul(bank(h % 4, 0, P), flip[:], skew[:, h, P:SEQ], start=True, stop=True)
                pe.matmul(bank(h % 4, P, SEQ), flip[:], skew[:, h, :], start=True, stop=True
                          ).then_inc(S["flip_done"], 1)

            for c in range(12):
                if c >= 4:
                    pe.wait_ge(S["evac"], EV_IN + c - 3)
                if c == 0:
                    first_chunks(chunk(0, 0), chunk(1, 0), 0)
                elif c > 1:
                    out_chunk(chunk(c % 4, 0))
                if c == 0:
                    pe.wait_ge(S["pool_const"], 4)
                    square_mean(6)
                    pe.wait_ge(S["consts_loaded"], 16 * len(consts))
                    pe.matmul(ps[0:HEADS, 7, 0:384], rel[:], strip, start=True, stop=True
                              ).then_inc(S["table_ready"], 1)
                if c == 2:
                    spread([(0, 6, SEQ), (1, 6, SEQ + P)])
            pe.wait_ge(S["skew_loaded"], 16)
            for i in range(4):
                token_unit(512, op_hi, op_lo, 2 * i, 2, i == 3)
                bias_tile(2 * i)
                bias_tile(2 * i + 1)
            pe.wait_ge(S["late_loaded"], 16 * len(late_consts))
            pe.wait_ge(S["pooled"], 1)
            for g in range(4):
                m = pe.matmul(chunk(6 + g // 2, g % 2), wpool[:, g, :], proj[:, g, :], start=True, stop=True)
            m.then_inc(S["pool_mixed"], 1)
            pe.wait_ge(S["evac"], EV_IN + 14)
            attention(
                HEADS,
                q=lambda h: proj[h % 2 * 64:h % 2 * 64 + 64, 4 + h // 2, :],
                k=lambda h: proj[h % 2 * 64:h % 2 * 64 + 64, 8 + h // 2, :],
                v=lambda h, t: vtok[:, t, h * 64:h * 64 + 64],
                o=lambda h: (h % 2 * 64, 4 + h // 2 if h % 2 == 0 else None),
                fillers=[[0], [1], [2], [(3, 0)], [(3, 1)], [(4, 0)], [(4, 1)], [(5, 0)], [(5, 1), (6, 0)], [(6, 1), 7]], mixed=lambda c: c + 1)
            mean_square(7)
            feed_forward(1, norm=True)
            mean_square(7)
            pe.wait_ge(S["acc_free"], 2)
            pe.wait_ge(S["p_split"], 1)
            for c in range(2):
                in_chunk(p_hi[:, c, :], p_lo[:, c, :], c == 0, c == 1, by_bank=False)
            for c in range(NCH):
                if c >= 4:
                    pe.wait_ge(S["sig_done"], c - 3)
                if c == 0:
                    first_chunks(chunk(5, 0), chunk(6, 0), 2)
                elif c > 1:
                    out_chunk(chunk(4 + (c + 1) % 4, 0))
            for c in range(17):
                if c >= 4:
                    pe.wait_ge(S["evac"], EV_EVEN + c - 3)
                if c == 0:
                    first_chunks(chunk(0, 0), chunk(1, 0), 3)
                elif c > 1:
                    out_chunk(chunk(c % 4, 0))
            token_unit(128, op_hi, op_lo, 0, 8, True)
            pe.wait_ge(S["evac"], EV_EVEN + 19)
            attention(
                HEADS,
                q=lambda h: proj[h % 2 * 64:h % 2 * 64 + 64, 12 + h // 2, :],
                k=lambda h: swa_k[h % 2 * 64:h % 2 * 64 + 64, :],
                v=lambda h, t: vtok[:, t, h % 2 * 64:h % 2 * 64 + 64],
                o=lambda h: (h % 2 * 64, 12 + h // 2 if h % 2 == 0 else None),
                fillers=[[0], [1], [2], [(3, 0)], [(3, 1)], [(4, 0)], [(4, 1)], [(5, 0)], [(5, 1), (6, 0)], [(6, 1), 7]], mixed=lambda c: c + 9)
            mean_over_features(4, y)
            mean_square(7)
            feed_forward(4)
            mean_over_features(4, y)
            mean_square(7)
            def level(i):
                b = level_bank[i]
                if i:
                    pe.wait_ge(S["decayed"], i)
                before = [j for j in range(i) if level_bank[j] == b]
                if before:
                    pe.wait_ge(S["level_kept"], before[-1] + 1)
                for a in range(2):
                    for t in range(2):
                        at = a * SEQ + t * P
                        if i:
                            mm = pe.matmul(bank(b + a, t * SEQ, SEQ), gk[:, i % 2, at:at + P],
                                           gq[i % 2][:, 2 * a + t, :, :], start=True, stop=True)
                            continue
                        for h in range(2):
                            r = slice(h * 64, h * 64 + 64)
                            mm = pe.matmul(bank(b + h, (2 * a + t) * P, P), proj[r, 6 + a, t * P:t * P + P],
                                           proj[r, 4 + a, t * P:t * P + P], start=True, stop=True)
                mm.then_inc(S["level_done"], 1)

            for c in range(12):
                if c >= 4:
                    pe.wait_ge(S["evac"], EV_ODD + c - 3)
                if c == 0:
                    first_chunks(chunk(0, 0), chunk(1, 0), 5)
                elif c > 1:
                    out_chunk(chunk(c % 4, 0))
                if c == 2:
                    pe.wait_ge(S["evac"], EV_ODD + 1)
                    for a in range(2):
                        m = pe.matmul(chunk(7, a), w_gate[:, a * P:a * P + P], proj[0:16, 2, :], start=True, stop=True)
                    m.then_inc(S["gate_z"], 1)
            pe.wait_ge(S["mla_sq"], 1)
            token_means(6, [(0, 1, [sq[:, 4, :], sq[:, 5, :]]), (2, 2, [sq[:, 6, :]])])
            pe.wait_ge(S["evac"], EV_ODD + 12)
            for i in range(4):
                token_unit(512, op_hi, op_lo, 2 * i, 2, i == 3)
                if i == 2:
                    pe.wait_ge(S["rinv_ready"], 1)
                    pe.wait_ge(S["gate_zb"], 1)
                level(i)
                if i == 0:
                    spread([(j, 6, j * P) for j in range(4)])
            level(4)
            level(5)
            s = take()
            pe.wait_ge(S["mla_split"], 1)
            pe.wait_ge(S["level_kept"], 4)
            for h in range(MLA_H):
                for k in range(2):
                    w = slice(k * 512 + h * P, k * 512 + h * P + P)
                    m = three(chunk(h // 2, h % 2), w_hi[:, s, w], w_lo[:, s, w], mix_hi[:, 4 + k, :],
                              mix_lo[:, 4 + k, :], k == 0, k == 1)
            given(m)
            level(6)
            s = take()
            pe.wait_ge(S["level_kept"], 5)
            pe.wait_ge(S["evac"], EV_ODD + 14)
            for h in range(MLA_H):
                w = slice(h * P, h * P + P)
                three(chunk(2 + h // 2, h % 2), w_hi[:, s, w], w_lo[:, s, w], mix_hi[:, 6, :], mix_lo[:, 6, :], True, True)
            for t in range(2):
                a, b = mix_hi[:, 6, t * P:t * P + P], mix_lo[:, 6, t * P:t * P + P]
                pe.matmul(bank(4 + t), a, w_hi[:, s, 512:1024], start=True, stop=False)
                pe.matmul(bank(4 + t), a, w_lo[:, s, 512:1024], start=False, stop=False)
                m = pe.matmul(bank(4 + t), b, w_hi[:, s, 512:1024], start=False, stop=True)
            given(m)
            pe.wait_ge(S["mla_evac"], 1)
            pe.wait_ge(S["rope_done"], 1)
            level(7)
            pe.wait_ge(S["mla_evac"], 3)

            def across():
                pe.wait_ge(S["decayed"], 8)
                pe.wait_ge(S["level_kept"], 7)
                for a in range(2):
                    m = pe.matmul(bank(6, a * SEQ, SEQ), gk[:, 0, a * SEQ:a * SEQ + P], gq[0][:, 2 * a + 1, :, :],
                                  start=True, stop=True)
                m.then_inc(S["level_done"], 1)

            def gla_values():
                pe.wait_ge(S["cross_kept"], 1)
                for h in range(GLA_H):
                    a, r = h // 2, h % 2
                    v0, v1 = vtok[:, 0, h * P:h * P + P], vtok[:, 1, h * P:h * P + P]
                    pe.matmul(bank(2 + a, r * SEQ, P), v0, att[:, r, 2 * a * P:2 * a * P + P], start=True, stop=True)
                    pe.matmul(bank(2 + a, r * SEQ + P, P), v1, att[:, r, (2 * a + 1) * P:(2 * a + 2) * P],
                              start=True, stop=False)
                    m = pe.matmul(bank(2 + a, r * SEQ + P, P), v0, cross[:, r, a * P:a * P + P], start=False, stop=True)
                m.then_inc(S["gla_out"], 1)

            def gla_statistic():
                pe.wait_ge(S["gla_sq"], 2)
                token_means(4, [(2 * h, 2, [sq[:, h, :]]) for h in range(GLA_H)])

            attention(
                MLA_H,
                q=lambda h: mq[0:MLA_QK, h, :], k=lambda h: mk[0:MLA_QK, h, :],
                v=lambda h, t: mv[:, t, h * P:h * P + P],
                o=lambda h: (0, 16 + h if h else None),
                fillers=[[], [], [], [(4, 0)], [(4, 1), (5, 0)], [(5, 1), 6, 7, 0, 1, 2, 3]],
                mixed=lambda c: 17 + c - 4 if c >= 4 else 22 if c < 2 else 24,
                between={0: across, 1: gla_values, 3: lambda: pe.wait_ge(S["gla_copied"], 1), 4: gla_statistic,
                         5: lambda: spread([(2 * h + t, 4 + h // 2, h % 2 * SEQ + t * P)
                                            for h in range(GLA_H) for t in range(2)])})
            mean_over_features(4, y)
            mean_square(7)
            feed_forward(6)
            mean_over_features(4, y)
            mean_square(7)
            assert unit.n == UNITS

        @block.scalar
        def _(act):
            own = Chain(act, S["act_step"])
            unit, split, head_count, hidden = (Cursor() for _ in range(4))

            def split_hi():
                s, turn = split.n % SLOTS, split.n // SLOTS
                act.wait_ge(raw_loaded[s], 16 * turn + 16 if split.turn is None else split.turn * 16 + (16 * turn + 16))
                if split.turn is not None or split.n >= SLOTS:
                    act.wait_ge(S["units_done"], split.at(1 - SLOTS))
                act.activation(w_hi[:, s, :], raw[:, s, :], ACT.Copy).then_inc(S["split_hi_done"], 1)
                split.n += 1

            def step(ahead=True):
                if ahead:
                    split_hi()
                unit.n += 1

            def unit_done():
                act.wait_ge(S["units_done"], unit.at())

            def acc_complete(b):
                if b < 3:
                    accs[0] += 1
                    act.wait_ge(S["acc_done"], accs[0])
                else:
                    unit_done()
            accs = [0]

            def squares(i, src):
                act.activation(pair(sq, i), src, ACT.Square).then_inc(S["sq_ready"], 1)

            def operand_hi(src, ready, gain=None):
                for i in range(4):
                    act.wait_ge(S[ready], seen[ready] + i + 1)
                    if gain is None:
                        m = act.activation(pair(op_hi, i), pair(src, i), ACT.Copy)
                    else:
                        for c in (2 * i, 2 * i + 1):
                            m = act.activation(op_hi[:, c, :], src[:, c, :], ACT.Copy, scale=vcol(gain, c))
                    m.then_inc(S["norm_hi"], 1)
                    if gain is not None:
                        squares(i, pair(src, i))
                seen[ready] += 4
            seen = {"x_ready": 0, "scaled": 0}

            def operand_hi_plus(shift, layer):
                for i in range(4):
                    act.wait_ge(S["scaled"], seen["scaled"] + i + 1)
                    for c in (2 * i, 2 * i + 1):
                        m = act.activation(op_hi[:, c, :], sq[:, c, :], ACT.Identity, bias=vcol(shift, layer * 8 + c))
                    m.then_inc(S["norm_hi"], 1)
                seen["scaled"] += 4

            def copy_out(dst, src, func=ACT.Copy, scale=1.0):
                act.activation(dst, src, func, scale=scale).then_inc(S["evac"], 1)

            def probs(g, sink=None):
                r = g % 2
                act.wait_ge(S["shift_ready"], g + 1)
                act.activation(logit[:, r, 0:P], logit[:, r, 0:P], ACT.Exp, bias=stat[:, r, 0:1],
                               accum_out=stat[:, r, 2:3])
                if sink is not None:
                    act.activation(stat[:, r, 6:8], stat[:, r, 0:2], ACT.Exp, bias=vcol("sinks", sink))
                act.activation(logit[:, r, P:384], logit[:, r, P:384], ACT.Exp, bias=stat[:, r, 1:2],
                               accum_out=stat[:, r, 3:4]).then_inc(S["probs_done"], 1)

            def attention(n, fillers, sink=None, between={}):
                h0 = head_count.n
                for t in range(n + 2):
                    if t >= 2:
                        g = h0 + t - 2
                        act.wait_ge(S["probT_done"], g + 1)
                        if g >= 2:
                            act.wait_ge(S["heads_done"], g - 1)
                        act.activation(probT[:, g % 2, :], bank(6, 0, 384), ACT.Copy).then_inc(S["probT_copied"], 1)
                    for _ in range(fillers[t]):
                        step()
                    if t < n:
                        probs(h0 + t, sink and sink(t))
                    if t in between:
                        between[t]()
                head_count.n += n

            def feed_forward(convolve, late=0):
                j0 = hidden.n

                def hidden_chunk(c, j, up=True):
                    step(ahead=not skip[0])
                    skip[0] -= skip[0] > 0
                    if not convolve:
                        unit_done()
                        act.activation(gate[:, c, :], chunk(4 + 2 * c, 0), ACT.Silu).then_inc(S["gate_act"], 1)
                    step(ahead=not skip[0])
                    skip[0] -= skip[0] > 0
                    if convolve:
                        act.wait_ge(S["conv_done"], j + 1)
                        act.activation(gate[:, c, :], conv[:, c, :], ACT.Gelu_apprx_tanh).then_inc(S["gate_act"], 1)

                skip = [late]
                hidden_chunk(0, 0)
                hidden_chunk(1, 1)
                step()
                hidden_chunk(0, 2)
                step()
                hidden_chunk(1, 3)
                turns = NFF // 2 - 2
                with act.Fori(0, turns) as i:
                    unit.enter(i, 6)
                    split.enter(i, 6)
                    step()
                    hidden_chunk(0, i * 2 + 4)
                    step()
                    hidden_chunk(1, i * 2 + 5)
                    unit.leave(turns)
                    split.leave(turns)
                step(ahead=not late)
                step(ahead=not late)
                hidden.n = j0 + NFF

            def layer_norm_squares():
                accs[0] += 3
                for i in range(4):
                    act.wait_ge(S["centred"], ln[0] * 4 + i + 1)
                    squares(i, pair(y, i))
                ln[0] += 1
            ln = [0]

            for name, ap in consts:
                act.dma_start(ap, d[name]).then_inc(S["consts_loaded"], 16)
            act.wait_ge(S["pool_const"], 1)
            own.done(act.activation(first[:], mean_w[:, 0, 0:1], ACT.Copy))
            act.wait_ge(S["vec_loaded"], 16)
            for i in range(4):
                act.wait_ge(x_loaded[i], 16)
                for c in (2 * i, 2 * i + 1):
                    m = act.activation(op_hi[:, c, :], x[:, c, :], ACT.Copy, scale=vcol("g_mix_pre", c))
                m.then_inc(S["norm_hi"], 1)
                if i == 0:
                    split_hi()
            for _ in range(3):
                split_hi()
            for i in range(4):
                squares(i, pair(x, i))
            for c in range(12):
                step()
            unit_done()
            for name, ap in late_consts:
                act.dma_start(ap, d[name]).then_inc(S["late_loaded"], 16)
            for i in range(4):
                step()
                for h in (2 * i, 2 * i + 1):
                    act.wait_ge(S["flip_done"], h + 1)
                    act.activation(bias[:, h, :], bank(h % 4, 0, 384), ACT.Copy).then_inc(S["bias_copied"], 1)
            unit_done()
            for t in range(2):
                copy_out(vtok[:, t, :], bank(4 + t), scale=tok_rinv[:, t:t + 1])
            attention(HEADS, [1, 1, 1, 0, 1, 0, 1, 0, 1, 2])

            for b in range(4):
                acc_complete(b)
                squares(b, bank2(b))
            operand_hi(x, "x_ready", gain="g_ffn_pre")
            act.wait_ge(S["late_loaded"], 16 * len(late_consts))
            act.activation(p_hi, pt[:], ACT.Copy).then_inc(S["p_hi_done"], 1)
            feed_forward(True)
            for b in range(4):
                acc_complete(b)
                squares(b, bank2(b))
            operand_hi(x, "x_ready")
            step()
            step()
            for c in range(NCH):
                step()
                unit_done()
                act.activation(sq[:, c, :], chunk(4 + (c + 1) % 4, 0), ACT.Sigmoid).then_inc(S["sig_done"], 1)
            operand_hi(x, "x_ready")
            for c in range(17):
                step()
                unit_done()
                copy_out(proj[:, c, :] if c < 16 else swa_k, chunk(c % 4, 0))
            step()
            unit_done()
            for t in range(2):
                copy_out(vtok[:, t, 0:P], bank(4 + t, 0, P))
            attention(HEADS, [1, 1, 1, 0, 1, 0, 1, 0, 1, 2], sink=lambda h: h // 2 + 4 * (h % 2))
            layer_norm_squares()
            operand_hi_plus("ln_mix_b", 0)
            feed_forward(False)
            layer_norm_squares()
            operand_hi_plus("ln_ffn_b", 0)
            def decay(i):
                act.wait_ge(S["decay_ready"], i)
                if i > 2:
                    act.wait_ge(S["decayed"], i - 2)
                act.activation(gee[:, i % 2, :], gdd[:, i % 2, :], ACT.Exp, scale=1.0 / GLA_TAU
                               ).then_inc(S["decay_exp"], 1)

            places = (2, 8, 9, 10, 11, 0, 1, 3)
            for c in range(12):
                step()
                if c < 8:
                    unit_done()
                    copy_out(proj[:, places[c], :], chunk(c % 4, 0), ACT.Silu if 1 <= c < 5 else ACT.Copy)
                if c == 4:
                    act.wait_ge(S["gate_zb"], 1)
                    own.done(act.activation(ge, gd, ACT.Abs))
                    own.settle()
                    own.done(act.activation(ge, ge, ACT.Exp, scale=-1.0))
                    own.settle()
                    act.activation(ge, ge, ACT.Ln, bias=1.0).then_inc(S["softplus_done"], 1)
                if c == 8:
                    act.wait_ge(S["evac"], EV_ODD + 8)
                    own.done(act.activation(sq[:, 4:6, :], proj[:, 0:2, :], ACT.Square))
                    act.activation(sq[:, 6, :], proj[:, 3, :], ACT.Square).then_inc(S["mla_sq"], 1)
                if c == 8:
                    decay(1)
            for i in range(2, 6):
                step()
                decay(i)
                if i == 4:
                    act.wait_ge(S["mla_normed"], 1)
                    act.activation(mix_hi[:, 4:7, :], y[:, 0:3, :], ACT.Copy).then_inc(S["mla_hi"], 1)
            unit_done()
            for t in range(2):
                copy_out(vtok[:, t, :], bank(4 + t))
            decay(6)
            decay(7)
            step()
            unit_done()
            for b in range(2):
                m = act.activation(mq[0:64, 2 * b:2 * b + 2, :], ps[0:64, b, :].rearrange("p (c t) -> p c t", c=2), ACT.Copy)
            m.then_inc(S["mla_evac"], 1)
            step()
            decay(8)
            unit_done()
            for b in range(2):
                m = act.activation(mk[0:64, 2 * b:2 * b + 2, :], ps[0:64, 2 + b, :].rearrange("p (c t) -> p c t", c=2), ACT.Copy)
            m.then_inc(S["mla_evac"], 1)
            for b in range(2):
                m = act.activation(mv[:, b, :], bank(4 + b), ACT.Copy)
            m.then_inc(S["mla_evac"], 1)

            def gla_leaves():
                act.wait_ge(S["gla_out"], 1)
                for a in range(2):
                    act.activation(pair(sq, a), bank2(2 + a), ACT.Square).then_inc(S["gla_sq"], 1)
                for a in range(2):
                    m = act.activation(gla_o[:, a, :], bank(2 + a), ACT.Copy)
                m.then_inc(S["gla_copied"], 1)
            attention(MLA_H, [0, 0, 0, 0, 1, 7], between={1: gla_leaves})
            layer_norm_squares()
            operand_hi_plus("ln_mix_b", 1)
            feed_forward(False, late=2)
            layer_norm_squares()
            for i in range(4):
                act.wait_ge(S["scaled"], seen["scaled"] + i + 1)
                for c in (2 * i, 2 * i + 1):
                    m = act.activation(x[:, c, :], sq[:, c, :], ACT.Identity, bias=vcol("ln_ffn_b", 8 + c))
                m.then_inc(S["result_ready"], 1)
            assert unit.n == UNITS and split.n == UNITS, (unit.n, split.n)

        @block.vector
        def _(dve):
            own = Chain(dve, S["dve_step"])
            unit, split, stats, hidden, head_count, ln = (Cursor() for _ in range(6))
            hi_n, means, acc_n = [0], [0], [0]

            def split_lo():
                s = split.n % SLOTS
                dve.wait_ge(S["split_hi_done"], split.at(1))
                dve.tensor_tensor(w_lo[:, s, :], raw[:, s, :], fp(w_hi[:, s, :]), ALU.subtract
                                  ).then_inc(S["split_done"], 1)
                split.n += 1

            def step(ahead=True):
                if ahead:
                    split_lo()
                unit.n += 1

            def unit_done():
                dve.wait_ge(S["units_done"], unit.at())

            def chained(ins):
                own.done(ins)
                own.settle()

            def acc_complete(b):
                if b < 3:
                    accs[0] += 1
                    dve.wait_ge(S["acc_done"], accs[0])
                else:
                    unit_done()
            accs = [0]

            def sum_squares(half):
                i = 2 * half
                sq_seen[0] += 2
                dve.wait_ge(S["sq_ready"], sq_seen[0])
                m = dve.tensor_tensor(pair(sq, i), pair(sq, i), pair(sq, i + 1), ALU.add)
                if half:
                    chained(m)
                    m = dve.tensor_tensor(sq[:, 4, :], sq[:, 4, :], sq[:, 5, :], ALU.add)
                m.then_inc(S["sq_summed"], 1)
            sq_seen = [0]

            def hand_statistic(b, eps, deferred=False):
                n = STATISTICS[stats.n]
                stats.n += 1
                dve.wait_ge(S["stat_done"], stats.n)
                if stats.n > 1:
                    dve.wait_ge(S["tok_rinv_ready"], stats.n - 1)
                mean = bank(b, 0, n)
                if deferred:
                    chained(dve.tensor_tensor(tok_var[:, 0:n], mean, tok_ffn[:], ALU.mult))
                    chained(dve.tensor_tensor(tok_var[:, 0:n], tok_var[:, 0:n], tok_ffn[:], ALU.mult))
                    mean = tok_var[:, 0:n]
                dve.tensor_scalar(tok_var[:, 0:n], mean, eps, None, ALU.add).then_inc(S["var_ready"], 1)

            def lo_piece(i, src):
                hi_n[0] += 1
                dve.wait_ge(S["norm_hi"], hi_n[0])
                if callable(src):
                    for c in (2 * i, 2 * i + 1):
                        m = src(c)
                else:
                    m = dve.tensor_tensor(pair(op_lo, i), pair(src, i), fp(pair(op_hi, i)), ALU.subtract)
                m.then_inc(S["operand_ready"], 1)

            def with_lo(piece, src):
                for i in range(4):
                    piece(i)
                    if i:
                        lo_piece(i - 1, src)
                lo_piece(3, src)

            def post_norm(gain, operand=None, deferred=False):
                def leave(b):
                    for c in (2 * b, 2 * b + 1):
                        m = dve.tensor_scalar(y[:, c, :], acc(c), vcol(gain, c), None, ALU.mult)
                    return m
                accs[0] += 3
                sum_squares(0)
                own.done(leave(0))
                sum_squares(1)
                for b in (1, 2):
                    own.done(leave(b))
                hand_statistic(7, RMS_EPS, deferred)
                leave(3).then_inc(S["acc_free"], 1)
                acc_n[0] += 1
                dve.wait_ge(S["acc_free"], acc_n[0])
                dve.wait_ge(S["spread_done"], stats.n)
                r = over(chunk(7, 1), 2)

                def piece(i):
                    chained(dve.tensor_tensor(pair(y, i), pair(y, i), r, ALU.mult))
                    dve.tensor_tensor(pair(x, i), pair(x, i), pair(y, i), ALU.add).then_inc(S["x_ready"], 1)

                def rest_of_gained(c):
                    return dve.scalar_tensor_tensor(op_lo[:, c, :], x[:, c, :], vcol(operand, c), fp(op_hi[:, c, :]),
                                                    ALU.mult, ALU.subtract)
                with_lo(piece, rest_of_gained if operand else x)
                if operand:
                    sum_squares(0)
                    sum_squares(1)

            def layer_norm(gain, shift, layer, final=False):
                for b in range(4):
                    acc_complete(b)
                    m = dve.scalar_tensor_tensor(pair(y, b), pair(x, b), ALPHA, bank2(b), ALU.mult, ALU.add)
                    if b < 2:
                        own.done(m)
                    else:
                        m.then_inc(S["z_ready"], 1)
                    if b == 1:
                        own.settle()
                        dve.tensor_tensor(pair(sq, 0), pair(y, 0), pair(y, 1), ALU.add).then_inc(S["z_ready"], 1)
                ln.n += 4
                means[0] += 1
                dve.wait_ge(S["z_ready"], 3 * means[0])
                dve.wait_ge(S["mean_done"], means[0])
                for i in range(4):
                    dve.tensor_tensor(pair(y, i), pair(y, i), over(chunk(4, 0), 2), ALU.subtract
                                      ).then_inc(S["centred"], 1)
                    if i == 2:
                        sum_squares(0)
                sum_squares(1)
                dve.wait_ge(S["centred"], ln.n)
                hand_statistic(7, LN_EPS)
                for c in range(NCH):
                    own.done(dve.tensor_scalar(y[:, c, :], y[:, c, :], vcol(gain, layer * 8 + c), None, ALU.mult))
                own.settle()
                dve.wait_ge(S["spread_done"], stats.n)
                r = over(chunk(7, 1), 2)

                def piece(i):
                    dve.tensor_tensor(pair(sq, i), pair(y, i), r, ALU.mult).then_inc(S["scaled"], 1)

                def rest(c):
                    return dve.scalar_tensor_tensor(op_lo[:, c, :], sq[:, c, :], vcol(shift, layer * 8 + c),
                                                    fp(op_hi[:, c, :]), ALU.add, ALU.subtract)

                def shifted(i):
                    for c in (2 * i, 2 * i + 1):
                        m = dve.tensor_scalar(x[:, c, :], sq[:, c, :], vcol(shift, layer * 8 + c), None, ALU.add)
                    return m

                if final:
                    for i in range(4):
                        piece(i)
                else:
                    with_lo(piece, rest)
                    for i in range(4):
                        own.done(shifted(i))
                    own.settle()

            def put_mix(c, n, src, hi_scale=None):
                hi, lo = mix_hi[:, c:c + n, :], mix_lo[:, c:c + n, :]
                chained(dve.tensor_copy(hi, src))
                dve.tensor_tensor(lo, src, fp(hi), ALU.subtract).then_inc(S["mix_ready"], n)

            def logits(g, tile, scale, sink):
                r = g % 2
                dve.wait_ge(S["scores_done"], g + 1)
                if g >= 2:
                    dve.wait_ge(S["probT_done"], g - 1)
                dve.scalar_tensor_tensor(logit[:, r, :], bank(4 + r, 0, 384), scale, tile, ALU.mult, ALU.add
                                         ).then_inc(S["logits_done"], 1)
                dve.wait_ge(S["logits_done"], g + 1)
                own.done(dve.reduce_max(stat[:, r, 0:1], logit[:, r, 0:P], AX_X))
                chained(dve.reduce_max(stat[:, r, 1:2], logit[:, r, P:384], AX_X))
                if sink is None:
                    m = dve.tensor_scalar(stat[:, r, 0:2], stat[:, r, 0:2], -1.0, None, ALU.mult)
                else:
                    m = dve.tensor_scalar(stat[:, r, 0:2], stat[:, r, 0:2], vcol("sinks", sink), -1.0, ALU.max, ALU.mult)
                m.then_inc(S["shift_ready"], 1)

            def normalise(g, sink):
                r = g % 2
                dve.wait_ge(S["probs_done"], g + 1)
                if sink is not None:
                    chained(dve.tensor_tensor(stat[:, r, 2:4], stat[:, r, 2:4], stat[:, r, 6:8], ALU.add))
                chained(dve.reciprocal(stat[:, r, 4:6], stat[:, r, 2:4]))
                own.done(dve.tensor_scalar(logit[:, r, 0:P], logit[:, r, 0:P], stat[:, r, 4:5], None, ALU.mult))
                dve.tensor_scalar(logit[:, r, P:384], logit[:, r, P:384], stat[:, r, 5:6], None, ALU.mult
                                  ).then_inc(S["probs_scaled"], 1)

            def attention(n, tile, scale, fillers, per_chunk, sink=None, between={}):
                h0 = head_count.n
                for t in range(n + 2):
                    if 1 <= t <= n:
                        normalise(h0 + t - 1, sink and sink(t - 1))
                    if t < n:
                        logits(h0 + t, tile(t), scale, sink and sink(t))
                    if t >= 2 and (t - 1) % per_chunk == 0:
                        dve.wait_ge(S["heads_done"], h0 + t - 1)
                        put_mix(4 + (t - 1) // per_chunk - 1, 1, ps[:, 7:8, 0:SEQ])
                    if t in between:
                        between[t]()
                    for _ in range(fillers[t]):
                        step()
                head_count.n += n

            def operand_scale():
                hand_statistic(0, RMS_EPS)
                step()
                step()
                dve.wait_ge(S["spread_done"], stats.n)
                dve.tensor_copy(rinv[:, 0:SEQ], chunk(0, 1)).then_inc(S["rinv_copied"], 1)
                dve.wait_ge(S["rinv_copied"], 1)

            def split_p():
                dve.wait_ge(S["p_hi_done"], 1)
                dve.tensor_tensor(p_lo, pt[:], fp(p_hi), ALU.subtract).then_inc(S["p_split"], 1)

            def feed_forward(convolve, late=0):
                j0 = hidden.n
                skip = [late]

                def wcol(at, j):
                    return vec[:, bass.ds(j + (VEC["conv_w"] + at), 1)] if not isinstance(j, int) else \
                        vec[:, j + VEC["conv_w"] + at:j + VEC["conv_w"] + at + 1]

                def hidden_chunk(c, j):
                    begins = convolve and isinstance(j, int) and j == 0
                    if begins:
                        operand_scale()
                    for part in range(2):
                        if not begins:
                            step(ahead=not skip[0])
                            skip[0] -= skip[0] > 0
                        if convolve and part == 0:
                            unit_done()
                            g = gate_n[:, c, :]
                            chained(dve.tensor_tensor(g, chunk(4 + 2 * c, 0), rinv[:, 0:SEQ], ALU.mult))
                            chained(dve.tensor_scalar(conv[:, c, :], g, wcol(2 * NFF, j), wcol(3 * NFF, j),
                                                      ALU.mult, ALU.add))
                            chained(dve.scalar_tensor_tensor(conv[:, c, 1:], g[:, 0:SEQ - 1], wcol(NFF, j),
                                                             conv[:, c, 1:], ALU.mult, ALU.add))
                            dve.scalar_tensor_tensor(conv[:, c, 2:], g[:, 0:SEQ - 2], wcol(0, j), conv[:, c, 2:],
                                                     ALU.mult, ALU.add).then_inc(S["conv_done"], 1)
                    unit_done()
                    dve.wait_ge(S["gate_act"], j + (j0 + 1))
                    chained(dve.tensor_tensor(h_fp[:, c, :], gate[:, c, :], chunk(5 + 2 * c, 0), ALU.mult))
                    chained(dve.tensor_copy(h_hi[:, c, :], h_fp[:, c, :]))
                    dve.tensor_tensor(h_lo[:, c, :], h_fp[:, c, :], fp(h_hi[:, c, :]), ALU.subtract
                                      ).then_inc(S["h_ready"], 1)

                hidden_chunk(0, 0)
                hidden_chunk(1, 1)
                if convolve:
                    split_p()
                step()
                hidden_chunk(0, 2)
                step()
                hidden_chunk(1, 3)
                turns, per = NFF // 2 - 2, 4 + 6 * convolve
                with dve.Fori(0, turns) as i:
                    unit.enter(i, 6)
                    split.enter(i, 6)
                    own.count.enter(i, per)
                    step()
                    hidden_chunk(0, i * 2 + 4)
                    step()
                    hidden_chunk(1, i * 2 + 5)
                    unit.leave(turns)
                    split.leave(turns)
                    own.count.leave(turns)
                step(ahead=not late)
                step(ahead=not late)
                hidden.n = j0 + NFF

            for i in range(4):
                hi_n[0] += 1
                dve.wait_ge(S["norm_hi"], hi_n[0])
                for c in (2 * i, 2 * i + 1):
                    m = dve.scalar_tensor_tensor(op_lo[:, c, :], x[:, c, :], vcol("g_mix_pre", c), fp(op_hi[:, c, :]),
                                                 ALU.mult, ALU.subtract)
                m.then_inc(S["operand_ready"], 1)
                if i == 0:
                    split_lo()
            for _ in range(3):
                split_lo()
            sum_squares(0)
            sum_squares(1)
            for c in range(16):
                step()
                if c == 0:
                    hand_statistic(6, RMS_EPS)
                    dve.wait_ge(S["table_ready"], 1)
                    dve.tensor_copy(table, ps[0:HEADS, 7, 0:384].rearrange("h (a b) -> h a b", a=2)
                                    ).then_inc(S["table_copied"], 1)
                    dve.wait_ge(S["spread_done"], 1)
                    chained(dve.tensor_copy(rinv[:, 0:SEQ], chunk(6, 1)))
                if c < 12:
                    unit_done()
                    dve.tensor_tensor(u_pad[:, c, 16:] if c < 4 else proj[:, c, :], chunk(c % 4, 0), rinv[:, 0:SEQ],
                                      ALU.mult).then_inc(S["evac"], 1)
                if c == 5:
                    dve.wait_ge(S["evac"], EV_IN + 4)
                    n = 16 + SEQ
                    chained(dve.tensor_tensor(pad_b[:, :, 1:n], u_pad[:, :, 1:n], u_pad[:, :, 0:n - 1], ALU.add))
                    chained(dve.tensor_tensor(pad_c[:, 1:4, 2:n], pad_b[:, 1:4, 2:n], pad_b[:, 1:4, 0:n - 2], ALU.add))
                if c == 6:
                    chained(dve.tensor_tensor(pad_b[:, 2:4, 4:n], pad_c[:, 2:4, 4:n], pad_c[:, 2:4, 0:n - 4], ALU.add))
                    chained(dve.tensor_tensor(pad_c[:, 3, 8:n], pad_b[:, 3, 8:n], pad_b[:, 3, 0:n - 8], ALU.add))
                if c == 7:
                    sums = [pad_b, pad_c, pad_b, pad_c]
                    for g in range(4):
                        own.done(dve.scalar_tensor_tensor(proj[:, g, :], sums[g][:, g, 16:], 0.5 ** (g + 1),
                                                          u_pad[:, g, 16:], ALU.mult, ALU.subtract))
                    own.settle()
                    for g in range(4):
                        own.done(dve.tensor_tensor(proj[:, g, 0:16], sums[g][:, g, 16:32], invc[:, g, :], ALU.mult))
                    own.settle()
                    dve.tensor_tensor(proj[:, 0:4, 0:16], proj[:, 0:4, 0:16], u_pad[:, :, 16:32], ALU.subtract
                                      ).then_inc(S["pooled"], 1)
            dve.wait_ge(S["pool_mixed"], 1)
            for g in range(4):
                src = chunk(6 + g // 2, g % 2)
                chained(dve.tensor_scalar(mix_hi[:, g, :], src, vcol("pool_scale", g), None, ALU.mult))
                dve.scalar_tensor_tensor(mix_lo[:, g, :], src, vcol("pool_scale", g), fp(mix_hi[:, g, :]),
                                         ALU.mult, ALU.subtract).then_inc(S["mix_ready"], 1)
            dve.wait_ge(S["bias_copied"], HEADS)
            attention(HEADS, lambda h: bias[:, h, :], DH ** -0.5, [1, 1, 1, 0, 1, 0, 1, 0, 1, 2], 2)
            post_norm("g_mix_post", operand="g_ffn_pre")
            feed_forward(True)
            post_norm("g_ffn_post", deferred=True)
            step()
            step()
            for c in range(NCH):
                step()
                dve.wait_ge(S["sig_done"], c + 1)
                chained(dve.tensor_tensor(sq[:, c, :], sq[:, c, :], acc(c), ALU.mult))
                m = dve.tensor_tensor(x[:, c, :], x[:, c, :], sq[:, c, :], ALU.add)
                if c % 2:
                    m.then_inc(S["x_ready"], 1)
            for i in range(4):
                lo_piece(i, x)
            for c in range(18):
                step()
                if c == 13:
                    dve.wait_ge(S["evac"], EV_EVEN + 12)
                    z = proj[:, 4:8, :]
                    chained(dve.tensor_tensor(z, z, proj[:, 8:12, :], ALU.mult))
                if c == 14:
                    for tap in (2, 1, 0):
                        for g in range(4):
                            w = vcol("ev_conv_w", 4 * tap + g)
                            if tap == 2:
                                m = dve.tensor_scalar(sq[:, g, :], z[:, g, :], w, None, ALU.mult)
                            else:
                                a = 2 - tap
                                m = dve.scalar_tensor_tensor(sq[:, g, a:], z[:, g, 0:SEQ - a], w, sq[:, g, a:],
                                                             ALU.mult, ALU.add)
                            own.done(m)
                        own.settle()
                if c == 15:
                    chained(dve.tensor_tensor(sq[:, 0:4, :], sq[:, 0:4, :], proj[:, 0:4, :], ALU.mult))
                if c == 16:
                    put_mix(0, 4, sq[:, 0:4, :])
            attention(HEADS, lambda h: masks[:, 1, :], DH ** -0.5, [1, 1, 1, 0, 1, 0, 1, 0, 1, 2], 2,
                      sink=lambda h: h // 2 + 4 * (h % 2))
            layer_norm("ln_mix_g", "ln_mix_b", 0)
            feed_forward(False)
            layer_norm("ln_ffn_g", "ln_ffn_b", 0)
            def decayed(i, m):
                dve.wait_ge(S["decay_exp"], i)
                if i == 1:
                    dve.wait_ge(S["pool_step"], 5)
                if i > 2:
                    dve.wait_ge(S["level_done"], i - 1)
                e = gee[:, i % 2, :]
                (ol, _), (el, _) = halves(gk[:, i % 2, :], m), halves(e, m)
                kl, _ = halves(proj[:, 6:8, :].rearrange("p a t -> p (a t)"), m)
                own.done(dve.tensor_tensor(ol, el, kl, ALU.mult))
                queries = proj[:, 4:6, :].rearrange("p a t -> p (a t)")
                for h in range(2):
                    r = slice(h * 64, h * 64 + 64)
                    if m <= 64:
                        dst = gq[i % 2][r, :, h, :].rearrange("p b (g k) -> p b g k", k=2 * m)[:, :, :, m:2 * m]
                        er, qr = (v[r, :].rearrange("p (b g k) -> p b g k", b=4, k=2 * m)[:, :, :, m:2 * m]
                                  for v in (e, queries))
                    else:
                        dst = gq[i % 2][r, :, h, :].rearrange("p (a t) k -> p a t k", t=2)[:, :, 1, :]
                        er, qr = (v[r, :].rearrange("p (a t k) -> p a t k", a=2, t=2)[:, :, 1, :] for v in (e, queries))
                    last = dve.tensor_tensor(dst, er, qr, ALU.mult)
                    if h == 0:
                        own.done(last)
                last.then_inc(S["decayed"], 1)

            def keep(i):
                dve.wait_ge(S["level_done"], i + 1)
                if i:
                    dve.wait_ge(S["level_kept"], i)
                mask = gmask[:, i, :].unsqueeze(1).unsqueeze(1).to_broadcast([P, 2, 2, P])
                into = att[:, :, :].rearrange("p h (a t k) -> p " + ("a t h k" if i else "h a t k"), a=2, t=2)
                for r in range(2):
                    m = dve.copy_predicated(into[:, r], mask,
                                            bank(level_bank[i] + r).rearrange("p (a b k) -> p a b k", a=2, b=2))
                    if r == 0:
                        own.done(m)
                m.then_inc(S["level_kept"], 1)

            lo_q, hi_q = slice(64, 96), slice(96, 128)
            cos, sin = rope[lo_q, :], rope[hi_q, :]
            turned_k = y[lo_q, 0:3, :]
            own.done(dve.memset(att, 0.0))
            for c in range(12):
                step()
                if c == 3:
                    dve.wait_ge(S["gate_z"], 1)
                    own.done(dve.tensor_scalar(gd[:, 0:SEQ], chunk(7, 0), vcol("b_gate", 0), None, ALU.add))
                    dve.tensor_scalar(gd[:, SEQ:512], chunk(7, 1), vcol("b_gate", 1), None, ALU.add
                                      ).then_inc(S["gate_zb"], 1)
                if c >= 8:
                    if c == 8:
                        dve.wait_ge(S["evac"], EV_ODD + 8)
                    unit_done()
                    dve.tensor_scalar(proj[:, c - 4, :], chunk(c % 4, 0), 0.125 if c < 10 else 1.0, None, ALU.mult
                                      ).then_inc(S["evac"], 1)
                if c == 5:
                    own.done(dve.tensor_tensor(turned_k[:, 0, :], proj[lo_q, 2, :], cos, ALU.mult))
                    chained(dve.tensor_tensor(turned_k[:, 1, :], proj[hi_q, 2, :], sin, ALU.mult))
                    chained(dve.tensor_tensor(turned_k[:, 2, :], turned_k[:, 0, :], turned_k[:, 1, :], ALU.add))
                    own.done(dve.tensor_copy(mk[lo_q, :, :], over(turned_k[:, 2, :], 4)))
                if c == 6:
                    dve.wait_ge(S["softplus_done"], 1)
                    chained(dve.scalar_tensor_tensor(gd, gd, 0.0, ge, ALU.min, ALU.subtract))
                    own.done(dve.tensor_tensor_scan(gb[:, 0:SEQ], scan0[:], gd[:, 0:SEQ], 0.0, ALU.mult, ALU.add))
                    dve.tensor_tensor_scan(gb[:, SEQ:512], scan0[:], gd[:, SEQ:512], 0.0, ALU.mult, ALU.add
                                           ).then_inc(S["gate_summed"], 1)
            hand_statistic(6, RMS_EPS)
            dve.wait_ge(S["evac"], EV_ODD + 12)
            for i in range(1, 7):
                if i < 5:
                    step()
                decayed(i, LEVELS[i])
                if i > 1:
                    keep(i - 2)
                if i == 2:
                    dve.wait_ge(S["spread_done"], stats.n)
                    dve.tensor_copy(rinv[:], bank(6)).then_inc(S["rinv_ready"], 1)
                    dve.wait_ge(S["rinv_ready"], 1)
                    for j in range(2):
                        own.done(dve.scalar_tensor_tensor(y[:, j, :], proj[:, j, :], vcol("q_g", j), rinv[:, 0:SEQ],
                                                          ALU.mult, ALU.mult))
                    dve.scalar_tensor_tensor(y[:, 2, :], proj[:, 3, :], vcol("kv_g", 0), rinv[:, SEQ:512],
                                             ALU.mult, ALU.mult).then_inc(S["mla_normed"], 1)
                if i == 4:
                    dve.wait_ge(S["mla_hi"], 1)
                    dve.tensor_tensor(mix_lo[:, 4:7, :], y[:, 0:3, :], fp(mix_hi[:, 4:7, :]), ALU.subtract
                                      ).then_inc(S["mla_split"], 1)
            step()
            decayed(7, LEVELS[7])
            keep(5)
            turned = sq[lo_q, 4:8, :]
            unit_done()
            for b in range(2):
                own.done(dve.tensor_tensor(mq[lo_q, 2 * b:2 * b + 2, :],
                                           ps[lo_q, b, :].rearrange("p (c t) -> p c t", c=2), over(cos, 2), ALU.mult))
                own.done(dve.tensor_tensor(turned[:, 2 * b:2 * b + 2, :],
                                           ps[hi_q, b, :].rearrange("p (c t) -> p c t", c=2), over(sin, 2), ALU.mult))
            own.settle()
            dve.tensor_tensor(mq[lo_q, :, :], mq[lo_q, :, :], turned, ALU.add).then_inc(S["rope_done"], 1)
            step()
            keep(6)
            decayed(8, 128)
            keep(7)

            def keep_across():
                dve.wait_ge(S["level_done"], 9)
                dve.tensor_copy(cross[:, :, :].rearrange("p h (a k) -> p a h k", a=2),
                                bank(6).rearrange("p (a h k) -> p a h k", a=2, h=2)).then_inc(S["cross_kept"], 1)

            def gla_norm_and_gate():
                dve.wait_ge(S["spread_done"], stats.n)
                dve.wait_ge(S["gla_copied"], 1)
                for a in range(2):
                    o, gr = gla_o[:, a, :], proj[:, 8 + 2 * a:10 + 2 * a, :].rearrange("p c t -> p (c t)")
                    chained(dve.scalar_tensor_tensor(o, o, vcol("gla_g", 0), bank(4 + a), ALU.mult, ALU.mult))
                    chained(dve.tensor_tensor(o, o, gr, ALU.mult))
                    put_mix(2 * a, 2, o.rearrange("p (c t) -> p c t", c=2))
            attention(MLA_H, lambda h: masks[:, 0, :], MLA_QK ** -0.5, [0, 0, 0, 0, 1, 7], 1,
                      between={0: keep_across, 4: lambda: hand_statistic(4, RMS_EPS), 5: gla_norm_and_gate})
            layer_norm("ln_mix_g", "ln_mix_b", 1)
            feed_forward(False, late=2)
            layer_norm("ln_ffn_g", "ln_ffn_b", 1, final=True)
            assert unit.n == UNITS and split.n == UNITS, (unit.n, split.n)


def units_of(w, per_chunk):
    k, n = w.shape
    t = w.reshape(k // P, P, n // P, P)
    if per_chunk == "out":
        return t.transpose(2, 1, 0, 3).reshape(n // P, P, k)
    return t.transpose(0, 1, 2, 3).reshape(k // P, P, n)


def token_units(w):
    k, n = w.shape
    per = UNIT // n
    return w.reshape(k // P // per, per, P, n).transpose(0, 2, 1, 3).reshape(-1, P, UNIT)


def feed_forward_units(w_gate, w_up, w_down):
    g, u, dn = units_of(w_gate, "out"), units_of(w_up, "out"), units_of(w_down, "in")
    order = [g[0], u[0], g[1], u[1]]
    for j in range(2, NFF):
        order += [dn[j - 2], g[j], u[j]]
    return np.stack(order + [dn[NFF - 2], dn[NFF - 1]])


def stream_of(i):
    zero = lambda k, n: np.zeros((k, n), np.float32)
    w = i["w_in"][0]
    parts = [units_of(w[:, 0:1536], "out"), token_units(w[:, 1536:]), units_of(i["w_out"][0], "in"),
             feed_forward_units(i["w_up"][0][:, :D_FF], i["w_up"][0][:, D_FF:], i["w_down"][0]),
             units_of(i["w_ple"][0], "in"), units_of(i["w_ple_gate"][0], "out")]
    pairs = np.concatenate([np.arange(h * 64, h * 64 + 64) for c in range(4) for h in (c, 4 + c)])
    w = i["ev_w_in_2"][0]
    parts += [units_of(np.concatenate([w[:, 0:1536], w[:, 1536:2048][:, pairs], w[:, 2048:2176]], 1), "out"),
              token_units(w[:, 2176:]),
              units_of(i["ev_w_out_2"][0][np.concatenate([np.arange(512), 512 + pairs])], "in"),
              feed_forward_units(i["ffn_w_gate_2"][0], i["ffn_w_up_2"][0], i["ffn_w_down_2"][0])]
    w = i["od_w_in_2"][0]
    gq, gk, gv, low, gr, cq, ckv, kr = np.split(w, np.cumsum([256, 256, 512, 16, 512, 256, 128])[:7], axis=1)
    turned = lambda t: np.concatenate([t[:, 16:], t[:, :16]], 1)
    misc = np.concatenate([low, zero(D, 48), kr, turned(kr)], 1)
    parts += [units_of(np.concatenate([misc, gr, cq, ckv, gq, gk], 1), "out"), token_units(gv)]
    uq, ukv = i["od_mla_w_uq_2"][0], i["od_mla_w_ukv_2"][0]
    q = [np.concatenate([uq[:, h * 96:h * 96 + 96], turned(uq[:, h * 96 + 64:h * 96 + 96])], 1) for h in range(MLA_H)]
    q = np.concatenate(q, 1)
    kk = [np.concatenate([ukv[:, h * 192:h * 192 + 64], zero(P, 64)], 1) for h in range(MLA_H)]
    vv = [ukv[:, h * 192 + 64:h * 192 + 192] for h in range(MLA_H)]
    parts += [np.concatenate([q[:P], q[P:]], 1)[None], np.concatenate(kk + vv, 1)[None],
              units_of(np.roll(i["od_w_out_2"][0], -512, axis=0), "in"),
              feed_forward_units(i["ffn_w_gate_2"][1], i["ffn_w_up_2"][1], i["ffn_w_down_2"][1])]
    return np.ascontiguousarray(np.concatenate(parts, 0))


def columns(v):
    return v.reshape(-1, P).T


def vectors_of(i):
    gla = i["od_gla_norm_g_2"][0]
    parts = [columns(i[n][0]) for n in ("g_mix_pre", "g_mix_post", "g_ffn_pre", "g_ffn_post", "pool_scale")]
    parts += [columns(i["conv_w"][0].reshape(-1)), columns(i["conv_b"][0]), columns(i["ev_conv_w_2"][0].reshape(-1))]
    parts += [columns(i[n].reshape(-1)) for n in ("ln_mix_g_2", "ln_mix_b_2", "ln_ffn_g_2", "ln_ffn_b_2",
                                                  "od_gla_b_gate_2", "od_gla_norm_g_2", "od_mla_q_norm_g_2",
                                                  "od_mla_kv_norm_g_2")]
    parts.append(np.tile(i["ev_sinks_2"].reshape(1, 8), (P, 1)))
    return np.ascontiguousarray(np.concatenate(parts, 1))


def constants():
    dist = 255 - np.arange(384)
    n = np.maximum(dist, 0)
    nf = np.maximum(n, 1).astype(np.float32)
    half = BUCKETS // 2
    large = half + (np.log(nf / np.float32(half)) / np.float32(math.log(MAX_DISTANCE / half)) * half).astype(np.int32)
    bucket = np.where(n < half, n, np.minimum(large, BUCKETS - 1))
    strip = np.zeros((BUCKETS + 1, 384), np.float32)
    strip[bucket, np.arange(384)] = dist >= 0
    strip[BUCKETS] = np.where(dist >= 0, 0.0, NEG)
    tok = np.arange(P)
    diag = np.where(tok[:, None] >= tok, 0.0, NEG)
    causal = np.concatenate([diag, np.zeros((P, P)), diag], 1)
    window = np.concatenate([diag, np.where(tok[:, None] < tok, 0.0, NEG), diag], 1)
    invc = np.stack([1.0 / np.minimum(np.arange(16) + 1, 2 ** (g + 1)) for g in range(4)])
    s, t = tok[:, None], tok[None, :]
    gmask = [(s == t)] + [(s // (2 * m) == t // (2 * m)) & (s % (2 * m) < m) & (t % (2 * m) >= m) for m in LEVELS[1:]]
    inv = np.float32(10000.0) ** (-np.arange(0, 32, 2, dtype=np.float32) / np.float32(32))
    ang = np.arange(SEQ, dtype=np.float32)[None, :] * inv.astype(np.float32)[:, None]
    cos, sin = np.cos(ang), np.sin(ang)
    rope = np.zeros((P, SEQ))
    rope[64:96] = np.concatenate([cos, cos])
    rope[96:128] = np.concatenate([-sin, sin])
    return {"strip": strip.reshape(BUCKETS + 1, 2, 192), "flip": np.eye(P)[::-1], "ident": np.eye(P),
            "invc": np.tile(invc[None], (P, 1, 1)), "masks": np.stack([causal, window], 1), "rope": rope,
            "gmask": np.stack(gmask, 1),
            "scan0": np.tile(((np.arange(SEQ) % GLA_CHUNK) != 0)[None], (P, 1))}


def features(v):
    return np.ascontiguousarray(v.T.reshape(-1, P, SEQ).transpose(1, 0, 2))


def arrays_of(i):
    a = {k: np.ascontiguousarray(v.astype(np.float32)) for k, v in constants().items()}
    a["stream"] = stream_of(i)
    a["x"] = features(i["x"][0])
    a["p"] = features(i["p"][0, 0])
    a["vec"] = vectors_of(i)
    a["rel"] = np.concatenate([i["rel_bias"], np.ones((1, HEADS), np.float32)], 0)
    a["wpool"] = np.ascontiguousarray(i["w_pool"][0].transpose(1, 0, 2))
    a["w_gate"] = i["od_gla_w_gate_2"][0]
    return a


def kernel(**inputs):
    import concourse.bacc as bacc
    from concourse.bass_utils import run_bass_kernel_spmd as run

    nc = bacc.Bacc("TRN2", target_bir_lowering=False, num_devices=1)
    arrays = arrays_of({k: np.asarray(v) for k, v in inputs.items()})
    d = {n: nc.dram_tensor(f"in_{n}", a.shape, mybir.dt.from_np(a.dtype), kind="ExternalInput").ap()
         for n, a in arrays.items()}
    out = nc.dram_tensor("result", (P, NCH, SEQ), F32, kind="ExternalOutput").ap()
    build(nc, d, out)
    r = run(nc, [{f"in_{n}": a for n, a in arrays.items()}], core_ids=[0])
    got = r.results[0]["result"]
    return np.ascontiguousarray(got.transpose(2, 1, 0).reshape(1, SEQ, D))
```
